# Optimizing a Trainium2 kernel written in Bass

```python
import math
import jax, jax.numpy as jnp
from jax import lax
import numpy as np

D_MODEL = 1024
BATCH = 1
SEQ = 1024
DEPTH = 1

HEAD_DIM = 64
NSA_HEADS = 8
NSA_KV_HEADS = 2
NSA_GROUP = NSA_HEADS // NSA_KV_HEADS
CMP_LEN = 32
CMP_STRIDE = 16
CMP_HIDDEN = 256
SEL_BLOCK = 64
SEL_TOPN = 16
NSA_WINDOW = 512
SEL_QBLK = 64
FORCE_SCORE = 1e4
DIL_PAIRS = ((128, 1), (512, 4), (2048, 16))
N_DIL_GROUPS = 3
DIL_HEADS_PER_GROUP = 4
DIL_HEADS = N_DIL_GROUPS * DIL_HEADS_PER_GROUP
QBLK = 128
NUM_BUCKETS = 32
REL_MAX_DIST = 2048
N_BIAS_HEADS = NSA_HEADS + DIL_HEADS
N_EXPERT_GROUPS = 4
EXPERTS_PER_GROUP = 8
N_EXPERTS = N_EXPERT_GROUPS * EXPERTS_PER_GROUP
TOPK_IN_GROUP = 2
D_EXPERT = 512
MOE_ROW_BLOCK = 256
RMS_EPS = 1e-6
NSA_Q_W = NSA_HEADS * HEAD_DIM
NSA_KV_W = 3 * 2 * NSA_KV_HEADS * HEAD_DIM
NSA_GATE_W = 3 * NSA_HEADS
DIL_QKV_W = 3 * DIL_HEADS * HEAD_DIM
MERGE_W = 2 * D_MODEL
IN_W = NSA_Q_W + NSA_KV_W + NSA_GATE_W + DIL_QKV_W + MERGE_W
IN_SPLITS = (NSA_Q_W, NSA_Q_W + NSA_KV_W, NSA_Q_W + NSA_KV_W + NSA_GATE_W,
             NSA_Q_W + NSA_KV_W + NSA_GATE_W + DIL_QKV_W)
NSA_OUT_W = NSA_HEADS * HEAD_DIM
DIL_OUT_W = DIL_HEADS_PER_GROUP * HEAD_DIM

kernel_name = "hybrid_nsa_dilated_hmoe_adaln"

def rmsnorm(x, g):
    xf = x.astype(jnp.float32)
    y = xf * lax.rsqrt(jnp.mean(xf * xf, axis=-1, keepdims=True) + RMS_EPS)
    return (y * g.astype(jnp.float32)).astype(x.dtype)

def t5_bucket(dist):
    dist = jnp.maximum(dist, 0)
    max_exact = NUM_BUCKETS // 2
    df = jnp.maximum(dist, 1).astype(jnp.float32)
    large = max_exact + (jnp.log(df / max_exact) / math.log(REL_MAX_DIST / max_exact)
                         * (NUM_BUCKETS - max_exact)).astype(jnp.int32)
    large = jnp.minimum(large, NUM_BUCKETS - 1)
    return jnp.where(dist < max_exact, dist, large)

def banded_attention(q, k, v, window, tbl, dist_scale):
    B, L, Hk, G, dh = q.shape
    nb = -(-L // QBLK)
    Lp = nb * QBLK
    P = -(-window // QBLK) * QBLK
    q = jnp.pad(q, ((0, 0), (0, Lp - L), (0, 0), (0, 0), (0, 0)))
    k = jnp.pad(k, ((0, 0), (P, Lp - L), (0, 0), (0, 0)))
    v = jnp.pad(v, ((0, 0), (P, Lp - L), (0, 0), (0, 0)))
    scale = dh ** -0.5

    def step(i):
        qs = i * QBLK
        qb = lax.dynamic_slice_in_dim(q, qs, QBLK, axis=1)
        kb = lax.dynamic_slice_in_dim(k, qs, QBLK + P, axis=1)
        vb = lax.dynamic_slice_in_dim(v, qs, QBLK + P, axis=1)
        s = jnp.einsum('bqhgd,bkhd->bhgqk', qb, kb).astype(jnp.float32) * scale
        tq = qs + jnp.arange(QBLK)
        tk = qs - P + jnp.arange(QBLK + P)
        dist = tq[:, None] - tk[None, :]
        valid = (dist >= 0) & (dist <= window) & (tk[None, :] >= 0)
        bias = jnp.transpose(tbl[t5_bucket(dist * dist_scale)], (2, 3, 0, 1)).astype(jnp.float32)
        s = jnp.where(valid, s + bias, -jnp.inf)
        m = jnp.max(s, axis=-1, keepdims=True)
        p = jnp.exp(s - m)
        den = jnp.sum(p, axis=-1, keepdims=True)
        o = jnp.einsum('bhgqk,bkhd->bqhgd', (p / den).astype(vb.dtype), vb)
        return o, (m + jnp.log(den))[..., 0]

    o, lse = lax.map(step, jnp.arange(nb))
    o = jnp.moveaxis(o, 0, 1).reshape(B, Lp, Hk, G, dh)[:, :L]
    lse = jnp.transpose(lse, (1, 0, 4, 2, 3)).reshape(B, Lp, Hk, G)[:, :L]
    return o, lse

def compress_blocks(k, pos, w1, w2):
    B, S, Hk, dh = k.shape
    nc = (S - CMP_LEN) // CMP_STRIDE + 1
    idx = jnp.arange(nc)[:, None] * CMP_STRIDE + jnp.arange(CMP_LEN)[None, :]
    blk = k[:, idx] + pos[None, None, :, None, :]
    blk = blk.transpose(0, 1, 3, 2, 4).reshape(B, nc, Hk, CMP_LEN * dh)
    return jax.nn.gelu(blk @ w1) @ w2

def nsa_compressed_selected(q, kc, vc, ks, vs, tbl):
    B, S, Hk, G, dh = q.shape
    nc = kc.shape[1]
    n_sel = S // SEL_BLOCK
    n_top = min(SEL_TOPN, n_sel)
    scale = dh ** -0.5
    c_start = jnp.arange(nc) * CMP_STRIDE
    c_end = c_start + CMP_LEN - 1
    s_start = jnp.arange(n_sel) * SEL_BLOCK
    overlap = jnp.clip(jnp.minimum(c_start[:, None] + CMP_LEN, s_start[None, :] + SEL_BLOCK)
                       - jnp.maximum(c_start[:, None], s_start[None, :]), 0).astype(jnp.float32) / CMP_STRIDE
    ks_blk = ks.transpose(0, 2, 1, 3).reshape(B, Hk, n_sel, SEL_BLOCK, dh)
    vs_blk = vs.transpose(0, 2, 1, 3).reshape(B, Hk, n_sel, SEL_BLOCK, dh)
    tbl_h = jnp.transpose(tbl, (1, 0, 2))
    bi = jnp.arange(B)[:, None, None, None]
    hi = jnp.arange(Hk)[None, :, None, None]
    blk_ids = jnp.arange(n_sel)

    def step(i):
        qs = i * SEL_QBLK
        qb = lax.dynamic_slice_in_dim(q, qs, SEL_QBLK, axis=1)
        t = qs + jnp.arange(SEL_QBLK)
        sc = jnp.einsum('bqhgd,bchd->bhgqc', qb, kc).astype(jnp.float32) * scale
        dist_c = t[:, None] - c_end[None, :]
        bias_c = jnp.transpose(tbl[t5_bucket(dist_c)], (2, 3, 0, 1)).astype(jnp.float32)
        sc = jnp.where(dist_c >= 0, sc + bias_c, -jnp.inf)
        m = jnp.max(sc, axis=-1, keepdims=True)
        m = jnp.where(jnp.isfinite(m), m, 0.0)
        pc = jnp.exp(sc - m)
        den = jnp.sum(pc, axis=-1, keepdims=True)
        pc = pc / jnp.where(den > 0, den, 1.0)
        o_c = jnp.einsum('bhgqc,bchd->bqhgd', pc.astype(vc.dtype), vc)
        imp = jnp.einsum('bhgqc,cn->bhqn', pc, overlap)
        jq = t // SEL_BLOCK
        forced = (blk_ids[None] == 0) | (blk_ids[None] == jq[:, None]) | (blk_ids[None] == jq[:, None] - 1)
        future = blk_ids[None] > jq[:, None]
        score = jnp.where(forced, FORCE_SCORE, jnp.where(future, -1.0, imp))
        _, idx = lax.top_k(score, n_top)
        ksel = ks_blk[bi, hi, idx].reshape(B, Hk, SEL_QBLK, n_top * SEL_BLOCK, dh)
        vsel = vs_blk[bi, hi, idx].reshape(B, Hk, SEL_QBLK, n_top * SEL_BLOCK, dh)
        pos = (idx[..., None] * SEL_BLOCK + jnp.arange(SEL_BLOCK)).reshape(B, Hk, SEL_QBLK, n_top * SEL_BLOCK)
        dist = t[None, None, :, None] - pos
        bias_s = jnp.moveaxis(tbl_h[hi, t5_bucket(dist)], -1, 2).astype(jnp.float32)
        ss = jnp.einsum('bqhgd,bhqkd->bhgqk', qb, ksel).astype(jnp.float32) * scale
        ss = jnp.where((dist >= 0)[:, :, None], ss + bias_s, -jnp.inf)
        ps = jax.nn.softmax(ss, axis=-1)
        o_s = jnp.einsum('bhgqk,bhqkd->bqhgd', ps.astype(vsel.dtype), vsel)
        return o_c, o_s

    o_c, o_s = lax.map(step, jnp.arange(S // SEL_QBLK))
    o_c = jnp.moveaxis(o_c, 0, 1).reshape(B, S, Hk, G, dh)
    o_s = jnp.moveaxis(o_s, 0, 1).reshape(B, S, Hk, G, dh)
    return o_c, o_s

def dilated_attention(q, k, v, tbl):
    B, S = q.shape[0], q.shape[1]
    outs, lses = [], []
    for g, (window, d) in enumerate(DIL_PAIRS):
        def sub(a):
            return a.reshape(B, S // d, d, *a.shape[2:]).swapaxes(1, 2).reshape(B * d, S // d, *a.shape[2:])
        o, lse = banded_attention(sub(q[:, :, g])[:, :, :, None], sub(k[:, :, g]), sub(v[:, :, g]),
                                  window // d, tbl[:, g, :, None], d)
        H, dh = o.shape[2], o.shape[4]
        outs.append(o[:, :, :, 0].reshape(B, d, S // d, H, dh).swapaxes(1, 2).reshape(B, S, H, dh))
        lses.append(lse[..., 0].reshape(B, d, S // d, H).swapaxes(1, 2).reshape(B, S, H))
    w = jax.nn.softmax(jnp.stack(lses, axis=0), axis=0)
    return jnp.sum(w[..., None] * jnp.stack(outs, axis=0).astype(jnp.float32), axis=0)

def hybrid_mixer(h, w_in, cmp_pos, cmp_w1, cmp_w2, w_up_nsa, w_up_dil, w_o, rel_bias):
    B, S, D = h.shape
    proj = h @ w_in
    q_n, kv_n, gate_n, qkv_d, merge = jnp.split(proj, IN_SPLITS, axis=-1)
    q_n = q_n.reshape(B, S, NSA_KV_HEADS, NSA_GROUP, HEAD_DIM)
    kv_n = kv_n.reshape(B, S, 3, 2, NSA_KV_HEADS, HEAD_DIM)
    gate_n = jax.nn.sigmoid(gate_n.astype(jnp.float32)).reshape(B, S, 3, NSA_KV_HEADS, NSA_GROUP)
    tbl_n = rel_bias[:, :NSA_HEADS].reshape(NUM_BUCKETS, NSA_KV_HEADS, NSA_GROUP)
    tbl_d = rel_bias[:, NSA_HEADS:].reshape(NUM_BUCKETS, N_DIL_GROUPS, DIL_HEADS_PER_GROUP)
    kc = compress_blocks(kv_n[:, :, 0, 0], cmp_pos[0], cmp_w1[0], cmp_w2[0])
    vc = compress_blocks(kv_n[:, :, 0, 1], cmp_pos[1], cmp_w1[1], cmp_w2[1])
    o_c, o_s = nsa_compressed_selected(q_n, kc, vc, kv_n[:, :, 1, 0], kv_n[:, :, 1, 1], tbl_n)
    o_w, _ = banded_attention(q_n, kv_n[:, :, 2, 0], kv_n[:, :, 2, 1], NSA_WINDOW, tbl_n, 1)
    o_nsa = (gate_n[:, :, 0, ..., None] * o_c + gate_n[:, :, 1, ..., None] * o_s
             + gate_n[:, :, 2, ..., None] * o_w).reshape(B, S, NSA_OUT_W).astype(h.dtype)
    qkv_d = qkv_d.reshape(B, S, 3, N_DIL_GROUPS, DIL_HEADS_PER_GROUP, HEAD_DIM)
    o_dil = dilated_attention(qkv_d[:, :, 0], qkv_d[:, :, 1], qkv_d[:, :, 2], tbl_d)
    o_dil = o_dil.reshape(B, S, DIL_OUT_W).astype(h.dtype)
    g_m = jax.nn.sigmoid(merge.astype(jnp.float32)).reshape(B, S, 2, D)
    merged = g_m[:, :, 0] * (o_nsa @ w_up_nsa) + g_m[:, :, 1] * (o_dil @ w_up_dil)
    return merged.astype(h.dtype) @ w_o

def hierarchical_moe(h, wg, bg, we, be, w1, w3, w2):
    B, S, D = h.shape
    T = B * S
    hf = h.reshape(T, D)
    lg = (hf @ wg).astype(jnp.float32) + bg.astype(jnp.float32)
    grp = jnp.argmax(lg, axis=-1)
    p_grp = jnp.take_along_axis(jax.nn.softmax(lg, axis=-1), grp[:, None], axis=-1)
    le = ((hf @ we).astype(jnp.float32) + be.astype(jnp.float32)).reshape(T, N_EXPERT_GROUPS, EXPERTS_PER_GROUP)
    le = jnp.take_along_axis(le, grp[:, None, None], axis=1)[:, 0]
    top_v, top_i = lax.top_k(le, TOPK_IN_GROUP)
    wts = jax.nn.softmax(top_v, axis=-1) * p_grp
    eid = (grp[:, None] * EXPERTS_PER_GROUP + top_i).astype(jnp.int32)
    N = T * TOPK_IN_GROUP
    e_flat = eid.reshape(-1)
    tok = jnp.repeat(jnp.arange(T, dtype=jnp.int32), TOPK_IN_GROUP)
    w_flat = wts.reshape(-1)
    order = jnp.argsort(e_flat)
    e_s, tok_s, w_s = e_flat[order], tok[order], w_flat[order]
    counts = jnp.bincount(e_flat, length=N_EXPERTS)
    pcounts = (counts + MOE_ROW_BLOCK - 1) // MOE_ROW_BLOCK * MOE_ROW_BLOCK
    pend = jnp.cumsum(pcounts)
    pstart = pend - pcounts
    start = jnp.cumsum(counts) - counts
    dest = pstart[e_s] + (jnp.arange(N) - start[e_s])
    nb = -(-N // MOE_ROW_BLOCK) + N_EXPERTS
    n_pad = nb * MOE_ROW_BLOCK
    xs = jnp.zeros((n_pad, D), h.dtype).at[dest].set(hf[tok_s])
    blk_e = jnp.clip(jnp.searchsorted(pend, jnp.arange(nb) * MOE_ROW_BLOCK, side='right'), 0, N_EXPERTS - 1)

    def expert_block(args):
        xb, e = args
        return (jax.nn.silu(xb @ w1[e]) * (xb @ w3[e])) @ w2[e]

    ys = lax.map(expert_block, (xs.reshape(nb, MOE_ROW_BLOCK, D), blk_e)).reshape(n_pad, D)
    out = jnp.zeros((T, D), h.dtype).at[tok_s].add((w_s[:, None] * ys[dest]).astype(h.dtype))
    return out.reshape(B, S, D)

def setup_inputs(seed: int = 0) -> dict:
    key = jax.random.key(seed)
    ks = jax.random.split(key, 24)

    def nrm(k, shape, s):
        return jax.random.normal(k, shape, jnp.float32) * s

    return {
        "x": nrm(ks[0], (BATCH, SEQ, D_MODEL), 1.0),
        "c": nrm(ks[1], (BATCH, D_MODEL), 1.0),
        "rel_bias": nrm(ks[2], (NUM_BUCKETS, N_BIAS_HEADS), 0.2),
        "ada_w": nrm(ks[3], (DEPTH, D_MODEL, 6 * D_MODEL), D_MODEL ** -0.5),
        "ada_b": nrm(ks[4], (DEPTH, 6 * D_MODEL), 0.01),
        "norm1": 1.0 + nrm(ks[5], (DEPTH, D_MODEL), 0.02),
        "norm2": 1.0 + nrm(ks[6], (DEPTH, D_MODEL), 0.02),
        "w_in": nrm(ks[7], (DEPTH, D_MODEL, IN_W), D_MODEL ** -0.5),
        "cmp_pos": nrm(ks[8], (DEPTH, 2, CMP_LEN, HEAD_DIM), 0.1),
        "cmp_w1": nrm(ks[9], (DEPTH, 2, CMP_LEN * HEAD_DIM, CMP_HIDDEN), (CMP_LEN * HEAD_DIM) ** -0.5),
        "cmp_w2": nrm(ks[10], (DEPTH, 2, CMP_HIDDEN, HEAD_DIM), CMP_HIDDEN ** -0.5),
        "w_up_nsa": nrm(ks[11], (DEPTH, NSA_OUT_W, D_MODEL), NSA_OUT_W ** -0.5),
        "w_up_dil": nrm(ks[12], (DEPTH, DIL_OUT_W, D_MODEL), DIL_OUT_W ** -0.5),
        "w_o": nrm(ks[13], (DEPTH, D_MODEL, D_MODEL), D_MODEL ** -0.5),
        "router_wg": nrm(ks[14], (DEPTH, D_MODEL, N_EXPERT_GROUPS), D_MODEL ** -0.5),
        "router_bg": nrm(ks[15], (DEPTH, N_EXPERT_GROUPS), 0.01),
        "router_we": nrm(ks[16], (DEPTH, D_MODEL, N_EXPERTS), D_MODEL ** -0.5),
        "router_be": nrm(ks[17], (DEPTH, N_EXPERTS), 0.01),
        "exp_w1": nrm(ks[18], (DEPTH, N_EXPERTS, D_MODEL, D_EXPERT), D_MODEL ** -0.5),
        "exp_w3": nrm(ks[19], (DEPTH, N_EXPERTS, D_MODEL, D_EXPERT), D_MODEL ** -0.5),
        "exp_w2": nrm(ks[20], (DEPTH, N_EXPERTS, D_EXPERT, D_MODEL), D_EXPERT ** -0.5),
        "norm_f": 1.0 + nrm(ks[21], (D_MODEL,), 0.02),
    }

def reference(x, c, rel_bias, ada_w, ada_b, norm1, norm2, w_in, cmp_pos, cmp_w1, cmp_w2,
              w_up_nsa, w_up_dil, w_o, router_wg, router_bg, router_we, router_be,
              exp_w1, exp_w3, exp_w2, norm_f):
    cond = jax.nn.silu(c)
    for l in range(DEPTH):
        mod = (cond @ ada_w[l] + ada_b[l])[:, None, :]
        sh1, sc1, g1, sh2, sc2, g2 = jnp.split(mod, 6, axis=-1)
        h = (rmsnorm(x, norm1[l]) * (1 + sc1) + sh1).astype(x.dtype)
        x = x + g1 * hybrid_mixer(h, w_in[l], cmp_pos[l], cmp_w1[l], cmp_w2[l],
                                  w_up_nsa[l], w_up_dil[l], w_o[l], rel_bias)
        h = (rmsnorm(x, norm2[l]) * (1 + sc2) + sh2).astype(x.dtype)
        x = x + g2 * hierarchical_moe(h, router_wg[l], router_bg[l], router_we[l], router_be[l],
                                      exp_w1[l], exp_w3[l], exp_w2[l])
    return rmsnorm(x, norm_f)


_drawn_inputs = setup_inputs


def setup_inputs(seed=0):
    import zlib

    import numpy as np

    out = dict(_drawn_inputs(seed))
    spreads = {}
    factors = {'norm1': 2.962,
     'router_bg': 60.8,
     'router_be': 13.49,
     'norm_f': 7.519,
     'norm2': 2.945,
     'cmp_pos': 3.398}
    for name, (base, spread) in spreads.items():
        noise = np.random.default_rng([zlib.crc32(name.encode()), seed]).standard_normal(out[name].shape)
        drawn = base * np.exp(spread * noise) if base else spread * noise
        out[name] = __import__('jax').numpy.asarray(drawn.astype(out[name].dtype))
    for name, factor in factors.items():
        out[name] = (out[name] * factor).astype(out[name].dtype)
    return out
```

```python
from contextlib import ExitStack

import numpy as np
import concourse.bass as bass
from concourse import mybir

ALU = mybir.AluOpType
ACT = mybir.ActivationFunctionType
F32 = mybir.dt.float32
I32 = mybir.dt.int32
U32 = mybir.dt.uint32
AX = mybir.AxisListType.X

P = 128
BANK = 512
D = 1024
KD = D // P
S = 1024
NT = S // P
DH = 64
NSA_H, NSA_KV = 8, 2
DIL_G, DIL_H = 3, 4
HEADS = NSA_H + DIL_G * DIL_H
BUCKETS = 32
NSA_WIN = 512
WIN_TILES = NSA_WIN // P + 1
CMP_LEN, CMP_STRIDE, CMP_HID = 32, 16, 256
NC = (S - CMP_LEN) // CMP_STRIDE + 1
LP = CMP_LEN // 2
DIL = ((128, 1), (512, 4), (2048, 16))
NG, EPG, NE = 4, 8, 32
DE = 512
KE = DE // P
MODS = 6 * KD
MAXBLK = 2 * S // P + NE
SCALE = DH ** -0.5
EPS = 1e-6
MASKED = -1.0e30
FLOOR = 1.0e20

C_Q = 0
C_KV = NSA_H * DH
C_SELV = C_KV + 3 * P
C_WINV = C_KV + 5 * P
C_GATE = C_KV + 6 * P
C_DIL = C_GATE + 3 * NSA_H
DILW = DIL_G * DIL_H * DH
C_MERGE = C_DIL + 3 * DILW
IN_W = C_MERGE + 2 * D

R_Q, R_CK, R_CV, R_SK, R_WK, R_DQ = 0, 512, 640, 768, 896, 1024
R_DK = R_DQ + DILW
R_ALL = R_DK + DILW

SEG, _at = {}, 0
for _name, _len in (("sel", 1152), ("win", 768), ("cmp", 2016), ("d0", 384), ("d1", 384), ("d2", 256)):
    SEG[_name] = (_at, _len)
    _at += _len
BIASW = _at

K_ID, K_TRI, K_ONE, K_E32, K_M128, K_G4, K_BLK, K_TOK = 0, 128, 256, 384, 416, 424, 428, 476
K_I128, K_B128 = 484, 612
K_W = 661


INPUTS = ("x", "c", "rel_bias", "ada_w", "ada_b", "norm1", "norm2", "w_in", "cmp_pos", "cmp_w1", "cmp_w2", "w_up_nsa",
          "w_up_dil", "w_o", "router_wg", "router_bg", "router_we", "router_be", "exp_w1", "exp_w3", "exp_w2",
          "norm_f")


def shape_constants():
    small = np.zeros((P, K_W), np.float32)
    small[:, K_ID:K_ID + P] = np.eye(P)
    small[:, K_TRI:K_TRI + P] = np.triu(np.ones((P, P)), 1)
    small[:, K_ONE:K_ONE + P] = 1
    small[:, K_E32:K_E32 + NE] = np.arange(NE)
    small[:, K_M128:K_M128 + NT] = P * np.arange(NT)
    small[:, K_G4:K_G4 + NG] = np.arange(NG)
    small[:, K_BLK:K_BLK + MAXBLK] = np.arange(MAXBLK)
    small[:, K_TOK:K_TOK + NT] = np.arange(S).reshape(NT, P).T

    small[:, K_I128:K_I128 + P] = np.arange(P)
    small[:, K_B128:K_B128 + MAXBLK + 1] = P * np.arange(MAXBLK + 1)

    def bucket(dist):
        exact = BUCKETS // 2
        far = exact + (np.log(np.maximum(dist, 1).astype(np.float32) / np.float32(exact))
                       / np.float32(np.log(2048 / exact)) * np.float32(exact)).astype(np.int32)
        return np.where(dist < exact, dist, np.minimum(far, BUCKETS - 1))

    def line(dist, most, step):
        ok = (dist >= 0) & (dist <= most)
        return np.where(ok, bucket(np.maximum(dist, 0) * step), BUCKETS)

    w = np.arange(2016)
    z, b = 63 - w % 126, w // 126
    rows = np.concatenate([
        line(1023 - np.arange(1152), S, 1),
        line(639 - np.arange(768), NSA_WIN, 1),
        line(CMP_STRIDE * z + b - (CMP_LEN - 1), S, 1),
        line(255 - np.arange(384), DIL[0][0] // DIL[0][1], DIL[0][1]),
        line(255 - np.arange(384), DIL[1][0] // DIL[1][1], DIL[1][1]),
        np.where((127 - np.arange(256)) % 2 == 0, line(127 - np.arange(256), 2 * DIL[2][0] // DIL[2][1],
                                                       DIL[2][1] // 2), BUCKETS),
    ])
    onehot = (np.arange(BUCKETS + 1)[:, None] == rows[None, :]).astype(np.float32)
    return small, onehot


class Count:

    def __init__(self, sem):
        self.sem, self.n = sem, 0

    def inc(self, instruction):
        instruction.then_inc(self.sem, 1)
        self.n += 1
        return self.n

    def wait(self, engine):
        engine.wait_ge(self.sem, self.n)


class Core:

    def __init__(self, nc, ctx, args):
        self.nc, self.ctx, self.stage, self.stage_sems = nc, ctx, ctx, []
        (self.x, self.c, self.rel_bias, self.ada_w, self.ada_b, self.norm1, self.norm2, self.w_in, self.cmp_pos,
         self.cmp_w1, self.cmp_w2, self.w_up_nsa, self.w_up_dil, self.w_o, self.router_wg, self.router_bg,
         self.router_we, self.router_be, self.exp_w1, self.exp_w3, self.exp_w2, self.norm_f, self.c_small,
         self.c_onehot, self.out) = (args[name] for name in INPUTS + ("c_small", "c_onehot", "out"))
        self.psum = ctx.enter_context(nc.psum_tensor("psum", [P, 8, BANK], F32))
        self.const = self.sbuf(ctx, "const", [P, K_W])
        self.ident = self.const[:, K_ID:K_ID + P]
        self.vecT = self.sbuf(ctx, "vecT", [P, 104])
        self.cond = self.sbuf(ctx, "cond", [P, KD])
        self.mod = self.sbuf(ctx, "mod", [P, MODS])
        self.modA = self.sbuf(ctx, "modA", [P, 2, KD])
        dram = lambda name, shape, dt=F32: nc.dram_tensor(name, shape, dt).ap()
        self.d_bias = dram("d_bias", (HEADS, BIASW))
        self.d_sel = dram("d_sel", (NSA_H, P, S))
        self.d_win = dram("d_win", (NSA_H, P, WIN_TILES * P))
        self.d_cmp = dram("d_cmp", (NSA_H, P, 120))
        self.d_dtab = dram("d_dtab", (DIL_G, DIL_H, P, 2 * P))
        self.d_qk = dram("d_qk", (R_ALL, S))
        self.d_dil = dram("d_dil", (DIL_G, S, DIL_H, DH + 2))
        self.d_xn = dram("d_xn", (S, D))
        self.d_y = dram("d_y", (MAXBLK * P, D))

    def sbuf(self, ctx, name, shape, dt=F32):
        return ctx.enter_context(self.nc.sbuf_tensor("sb_" + name, shape, dt))

    def sem(self, name):
        sem = self.stage.enter_context(self.nc.semaphore(name))
        self.stage_sems.append(sem.num)
        return sem

    def block(self, mem):
        mem.callback(self.clear_semaphores, tuple(self.stage_sems))
        self.stage_sems.clear()
        return mem.enter_context(self.nc.Block())

    def clear_semaphores(self, numbers):
        with self.nc.Block() as block:
            @block.gpsimd
            def _(pool):
                first = min(numbers)
                while first <= max(numbers):
                    last = first
                    while last + 1 in numbers:
                        last += 1
                    pool.sem_clear(range(first, last + 1))
                    first = min([n for n in numbers if n > last], default=last + 1)


def settle(eng, passed):
    eng.sem_inc(passed, 1)


def load_mod_weights(eng, k, ada, slot, group, loaded):
    eng.dma_start(ada[:, slot], k.ada_w[0].rearrange("(k p) n -> p k n", p=P)[:, :, group * BANK:(group + 1) * BANK]
                  ).then_inc(loaded, 16)


def mod_products(eng, k, ada, slot, acc, count, before, passed=None):
    for kk in range(KD):
        if kk:
            eng.wait_ge(count, before + kk)
        if passed is not None:
            settle(eng, passed)
        c = k.cond[:, kk:kk + 1]
        (eng.scalar_tensor_tensor(acc, ada[:, slot, kk, :], c, acc, ALU.mult, ALU.add) if kk else
         eng.tensor_scalar(acc, ada[:, slot, 0, :], c, None, ALU.mult)).then_inc(count, 1)


def mod_columns(pe, k, acc, bank, n, done):
    for j in range(n):
        mm = pe.matmul(k.psum[:, bank, j:j + 1], acc[:, j * P:(j + 1) * P], k.const[:, K_ONE:K_ONE + 1],
                       start=True, stop=True)
    mm.then_inc(done, 1)


def stage_condition_and_norm(k, hT):
    nc = k.nc
    with ExitStack() as mem:
        k.stage = mem
        sb = lambda n, s, d=F32: k.sbuf(mem, "a_" + n, s, d)
        vec = sb("vec", [104, P])
        relb = sb("relb", [BUCKETS + 1, HEADS])
        onehot = sb("onehot", [BUCKETS + 1, BIASW])
        brow = sb("brow", [HEADS, BIASW])
        xs = sb("xs", [P, NT, D])
        sq = sb("sq", [P, 2, D])
        ss, var, std, rstd = (sb(n, [P, NT]) for n in ("ss", "var", "std", "rstd"))
        ada = sb("ada", [P, 4, KD, BANK])
        acc = sb("acc", [P, 4 * BANK])
        s_vec, s_const, s_oh, s_brow_out = (k.sem("a_" + n) for n in ("vec", "const", "onehot", "brow_out"))
        s_x = [k.sem(f"a_x{i}") for i in range(4)]
        s_ada = [k.sem(f"a_ada{i}") for i in range(4)]
        (s_mask, s_vecps, s_vecT, s_cond, s_bps, s_brow, s_ss, s_var, s_std, s_rstd, s_xn, s_tr, s_evd, s_eva,
         s_acc, s_mod, s_modA, s_out) = (k.sem("a_" + n) for n in (
             "mask", "vecps", "vecT", "cond", "bias_ps", "brow", "ss", "var", "std", "rstd", "xn", "transposed",
             "evac_dve", "evac_act", "acc", "mod", "modA", "modulated"))
        nbias = -(-BIASW // BANK)
        bias_cols = [slice(i * BANK, min(BIASW, (i + 1) * BANK)) for i in range(nbias)]
        block = k.block(mem)

        @block.sync
        def _(sp):
            vw = lambda ap: ap.rearrange("a (k p) -> (a k) p", p=P)
            sp.dma_start(vec[0:8, :], vw(k.c)).then_inc(s_vec, 16)
            sp.dma_start(vec[8:16, :], vw(k.norm1)).then_inc(s_vec, 16)
            sp.dma_start(vec[16:24, :], vw(k.norm2)).then_inc(s_vec, 16)
            sp.dma_start(vec[24:72, :], vw(k.ada_b)).then_inc(s_vec, 16)
            sp.dma_start(vec[72:104, :], k.cmp_pos[0].rearrange("a (l two) d -> (a l) (two d)", two=2)
                         ).then_inc(s_vec, 16)
            xv = k.x[0].rearrange("(t p) d -> p t d", p=P)
            for i in range(4):
                sp.dma_start(xs[:, 2 * i:2 * i + 2, :], xv[:, 2 * i:2 * i + 2, :]).then_inc(s_x[i], 16)
            for g in range(4):
                load_mod_weights(sp, k, ada, g, g, s_ada[g])
            sp.wait_ge(s_brow, nbias)
            sp.dma_start(k.d_bias, brow[:, :]).then_inc(s_brow_out, 16)
            sp.wait_ge(s_brow_out, 16)

        @block.gpsimd
        def _(pool):
            pool.memset(relb[BUCKETS:BUCKETS + 1, :], MASKED).then_inc(s_mask, 1)

        @block.scalar
        def _(act):
            act.dma_start(k.const[:, :], k.c_small).then_inc(s_const, 16)
            act.dma_start(relb[0:BUCKETS, :], k.rel_bias).then_inc(s_oh, 16)
            act.dma_start(onehot[:, :], k.c_onehot).then_inc(s_oh, 16)
            act.wait_ge(s_vecT, 1)
            act.activation(k.cond[:, :], k.vecT[:, 0:8], ACT.Silu).then_inc(s_cond, 1)
            for i in range(4):
                act.wait_ge(s_x[i], 16)
                for t in (2 * i, 2 * i + 1):
                    if t >= 2:
                        act.wait_ge(s_ss, t - 1)
                    act.activation(sq[:, t % 2, :], xs[:, t, :], ACT.Square, accum_out=ss[:, t:t + 1]
                                   ).then_inc(s_ss, 1)
                act.wait_ge(s_var, i + 1)
                act.activation(std[:, 2 * i:2 * i + 2], var[:, 2 * i:2 * i + 2], ACT.Sqrt).then_inc(s_std, 1)
                for t in (2 * i, 2 * i + 1):
                    act.wait_ge(s_tr, 2 * t + 2)
                    act.copy(hT[:, 4:8, t * P:(t + 1) * P],
                             k.psum[:, 4 + (2 * t + 1) % 4, :].rearrange("p (k c) -> p k c", k=4)).then_inc(s_eva, 1)
            for i, cols in enumerate(bias_cols):
                act.wait_ge(s_bps, i + 1)
                act.copy(brow[:, cols], k.psum[0:HEADS, 2 + i % 2, 0:cols.stop - cols.start]).then_inc(s_brow, 1)
            act.wait_ge(s_modA, 2)
            act.wait_ge(s_eva, NT)
            act.wait_ge(s_evd, NT)
            for kk in range(5, KD):
                act.activation(hT[:, kk, :], hT[:, kk, :], ACT.Identity, scale=k.modA[:, 0, kk:kk + 1],
                               bias=k.mod[:, kk:kk + 1]).then_inc(s_out, 1)

        @block.vector
        def _(dve):
            dve.wait_ge(s_vecps, 1)
            dve.tensor_copy(k.vecT[:, :], k.psum[:, 0, 0:104]).then_inc(s_vecT, 1)
            for i in range(4):
                two = slice(2 * i, 2 * i + 2)
                dve.wait_ge(s_ss, 2 * i + 2)
                dve.tensor_scalar(var[:, two], ss[:, two], 1.0 / D, EPS, ALU.mult, ALU.add).then_inc(s_var, 1)
                dve.wait_ge(s_std, i + 1)
                dve.reciprocal(rstd[:, two], std[:, two]).then_inc(s_rstd, 1)
                dve.wait_ge(s_rstd, i + 1)
                for t in (2 * i, 2 * i + 1):
                    dve.tensor_scalar(xs[:, t, :], xs[:, t, :], rstd[:, t:t + 1], None, ALU.mult).then_inc(s_xn, 1)
                for t in (2 * i, 2 * i + 1):
                    dve.wait_ge(s_tr, 2 * t + 1)
                    dve.tensor_copy(hT[:, 0:4, t * P:(t + 1) * P],
                                    k.psum[:, 4 + (2 * t) % 4, :].rearrange("p (k c) -> p k c", k=4)).then_inc(s_evd, 1)
            dve.wait_ge(s_cond, 1)
            for g in range(4):
                dve.wait_ge(s_ada[g], 16)
                mod_products(dve, k, ada, g, acc[:, g * BANK:(g + 1) * BANK], s_acc, KD * g)
            dve.wait_ge(s_mod, 1)
            dve.tensor_tensor(k.mod[:, 0:16], k.psum[:, 1, 0:16], k.vecT[:, 24:40], ALU.add).then_inc(s_modA, 1)
            dve.wait_ge(s_modA, 1)
            dve.scalar_tensor_tensor(k.modA[:, 0, :], k.mod[:, 8:16], 1.0, k.vecT[:, 8:16], ALU.add, ALU.mult
                                     ).then_inc(s_modA, 1)
            dve.wait_ge(s_modA, 2)
            dve.wait_ge(s_evd, NT)
            dve.wait_ge(s_eva, NT)
            for kk in range(5):
                dve.tensor_scalar(hT[:, kk, :], hT[:, kk, :], k.modA[:, 0, kk:kk + 1], k.mod[:, kk:kk + 1],
                                  ALU.mult, ALU.add).then_inc(s_out, 1)

        @block.tensor
        def _(pe):
            pe.wait_ge(s_vec, 80)
            pe.wait_ge(s_const, 16)
            pe.transpose(k.psum[:, 0, 0:104], vec[:, :], k.ident[0:104, 0:104]).then_inc(s_vecps, 1)
            for c in range(2 * NT):
                t, half = divmod(c, 2)
                pe.wait_ge(s_xn, t + 1)
                if c >= 4:
                    pe.wait_ge(s_eva if half else s_evd, (c - 4) // 2 + 1)
                for j in range(4):
                    d0 = (4 * half + j) * P
                    tr = pe.transpose(k.psum[:, 4 + c % 4, j * P:(j + 1) * P], xs[:, t, d0:d0 + P], k.ident)
                tr.then_inc(s_tr, 1)
            pe.wait_ge(s_oh, 32)
            pe.wait_ge(s_mask, 1)
            for i, cols in enumerate(bias_cols):
                if i >= 2:
                    pe.wait_ge(s_brow, i - 1)
                pe.matmul(k.psum[0:HEADS, 2 + i % 2, 0:cols.stop - cols.start], relb[:, :], onehot[:, cols],
                          start=True, stop=True).then_inc(s_bps, 1)
            pe.wait_ge(s_acc, 4 * KD)
            mod_columns(pe, k, acc, 1, 16, s_mod)


RUNS = (
    (C_Q, P, R_Q, 2, SCALE),
    (C_KV, P, R_CK, 1, 1.0),
    (C_KV + 2 * P, 2 * P, R_SK, 1, 1.0),
    (C_DIL, P, R_DQ, 3, SCALE),
    (C_DIL + DILW, P, R_DK, 3, 1.0),
)
RV = 2 * P + 3 * NSA_H


def dilated_tokens(group, slot):
    if group == 0:
        return lambda h: h[:, slot * P:(slot + 1) * P]
    if group == 1:
        r, b = divmod(slot, 2)
        return lambda h: h[:, 512 * b + r:512 * b + r + 509:4]
    return lambda h: h[:, slot:slot + 8 * (P - 1) + 1:8]


def spread_bias(eng, k, s_tab):
    rows = lambda seg, head, start, dims: bass.AP(k.d_bias.tensor, head * BIASW + SEG[seg][0] + start, dims)
    n = 0
    for dst, seg, head, heads, w in ((k.d_sel, "sel", 0, NSA_H, S), (k.d_win, "win", 0, NSA_H, WIN_TILES * P),
                                     (k.d_dtab[0], "d0", 8, DIL_H, 2 * P), (k.d_dtab[1], "d1", 12, DIL_H, 2 * P),
                                     (k.d_dtab[2][:, :, 0:P], "d2", 16, DIL_H, P)):
        eng.dma_start(dst, rows(seg, head, P - 1, [[BIASW, heads], [-1, P], [1, w]])).then_inc(s_tab, 16)
        n += 16
    for h in range(NSA_H):
        eng.dma_start(k.d_cmp[h].rearrange("(a b) v -> b a v", a=8)[:, :, 0:119],
                      rows("cmp", h, 7, [[126, 16], [-1, 8], [1, 119]])).then_inc(s_tab, 16)
        n += 16
    return n


def stage_projections(k, hT, vA, vD, gates, w1c, w2c, s_cw):
    nc = k.nc
    with ExitStack() as mem:
        k.stage = mem
        sb = lambda n, s, d=F32: k.sbuf(mem, "b_" + n, s, d)
        wq = [sb(f"wq{i}", [P, KD, P]) for i in range(2)]
        stage = [sb(f"stage{i}", [P, 2, BANK]) for i in range(2)]
        wva = sb("wva", [P, KD, RV])
        wvd = sb("wvd", [P, DIL_G, KD, 256])
        s_w = [k.sem(f"b_w{i}") for i in range(2)]
        s_store = [k.sem(f"b_store{i}") for i in range(2)]
        s_tab = k.sem("b_tables")
        s_wv = [k.sem(f"b_wv{i}") for i in range(4)]
        s_h0, s_h1, s_eva, s_evd, s_v, s_va, s_vd = (k.sem("b_" + n) for n in (
            "half0_ps", "half1_ps", "half0_out", "half1_out", "v_ps", "v_act", "v_dve"))
        w_in = k.w_in[0].rearrange("(k p) n -> p k n", p=P)
        pairs_before = [sum(r[3] for r in RUNS[:i]) for i in range(len(RUNS))]
        npairs = sum(r[3] for r in RUNS)
        vjobs = [(s, t) for s in range(4) for t in range(NT)]
        block = k.block(mem)

        @block.sync
        def _(sp):
            for run, (col, gap, row, n, scale) in enumerate(RUNS):
                with sp.Fori(0, n) as i:
                    g = i + pairs_before[run]
                    for s in range(2):
                        sp.wait_ge(s_h1, 2 * g + (s + 1))
                        sp.dma_start(wq[s][:, :, :], w_in[:, :, bass.ds(i * (2 * P) + (col + gap * s), P)]
                                     ).then_inc(s_w[s], 16)
            for s in range(2):
                sp.wait_ge(s_store[s], 16 * (npairs + 1))

        @block.gpsimd
        def _(pool):
            pool.wait_ge(s_tab, spread_bias(pool, k, s_tab))

        @block.scalar
        def _(act):
            act.sem_inc(s_eva, 2)
            for s in range(2):
                act.sem_inc(s_store[s], 16)
            for run, (col, gap, row, n, scale) in enumerate(RUNS):
                if run == 1:
                    act.dma_start(wva[:, :, 0:P], w_in[:, :, C_SELV:C_SELV + P]).then_inc(s_wv[0], 16)
                    act.dma_start(wva[:, :, P:RV], w_in[:, :, C_WINV:C_GATE + 3 * NSA_H]).then_inc(s_wv[0], 16)
                    for g in range(DIL_G):
                        c0 = C_DIL + 2 * DILW + 256 * g
                        act.dma_start(wvd[:, g], w_in[:, :, c0:c0 + 256]).then_inc(s_wv[g + 1], 16)
                if run == 3:
                    for kv in range(2):
                        act.dma_start(w1c[:, kv], k.cmp_w1[0, kv].rearrange("(l p) n -> p l n", p=P)).then_inc(s_cw, 16)
                        act.dma_start(w2c[:, kv], k.cmp_w2[0, kv].rearrange("(c p) n -> p c n", p=P)).then_inc(s_cw, 16)
                with act.Fori(0, n) as i:
                    g = i + pairs_before[run]
                    for s in range(2):
                        act.wait_ge(s_h0, 2 * g + (s + 1))
                        act.wait_ge(s_store[s], 16 * g + 16)
                        act.activation(stage[s][:, 0, :], k.psum[:, 2 * s, :], ACT.Copy, scale=scale
                                       ).then_inc(s_eva, 1)
                        act.wait_ge(s_eva, 2 * g + (s + 3))
                        act.wait_ge(s_evd, 2 * g + (s + 3))
                        act.dma_start(k.d_qk[bass.ds(i * (2 * P) + (row + P * s), P), :],
                                      stage[s][:, :, :].rearrange("p a b -> p (a b)")).then_inc(s_store[s], 16)
            for n, (s, t) in enumerate(vjobs):
                if n % 2 == 0:
                    act.wait_ge(s_v, n + 1)
                    dst = vA[:, t, :] if s == 0 else vD[:, s - 1, t, :]
                    act.copy(dst, k.psum[:, 4 + n % 4, 0:dst.shape[-1]]).then_inc(s_va, 1)
            act.wait_ge(s_va, len(vjobs) // 2)
            act.wait_ge(s_vd, len(vjobs) // 2)
            act.activation(gates[:, :, :], vA[:, :, 2 * P:RV], ACT.Sigmoid).then_inc(s_va, 1)

        @block.vector
        def _(dve):
            dve.sem_inc(s_evd, 2)
            for run, (col, gap, row, n, scale) in enumerate(RUNS):
                with dve.Fori(0, n) as i:
                    g = i + pairs_before[run]
                    for s in range(2):
                        dve.wait_ge(s_h1, 2 * g + (s + 3))
                        dve.wait_ge(s_store[s], 16 * g + 16)
                        dve.tensor_scalar(stage[s][:, 1, :], k.psum[:, 2 * s + 1, :], scale, None, ALU.mult
                                          ).then_inc(s_evd, 1)
            for n, (s, t) in enumerate(vjobs):
                if n % 2 == 1:
                    dve.wait_ge(s_v, n + 1)
                    dst = vA[:, t, :] if s == 0 else vD[:, s - 1, t, :]
                    dve.tensor_copy(dst, k.psum[:, 4 + n % 4, 0:dst.shape[-1]]).then_inc(s_vd, 1)

        @block.tensor
        def _(pe):
            pe.sem_inc(s_h1, 2)
            for run, (col, gap, row, n, scale) in enumerate(RUNS):
                with pe.Fori(0, n) as i:
                    g = i + pairs_before[run]
                    for s in range(2):
                        pe.wait_ge(s_w[s], 16 * g + 16)
                        for half in range(2):
                            pe.wait_ge(s_evd if half else s_eva, 2 * g + (s + 1))
                            for kk in range(KD):
                                mm = pe.matmul(k.psum[:, 2 * s + half, :], wq[s][:, kk, :],
                                               hT[:, kk, half * BANK:(half + 1) * BANK],
                                               start=(kk == 0), stop=(kk == KD - 1))
                            mm.then_inc(s_h1 if half else s_h0, 1)
            for n, (s, t) in enumerate(vjobs):
                if t == 0:
                    pe.wait_ge(s_wv[s], 32 if s == 0 else 16)
                if n >= 4:
                    pe.wait_ge(s_vd if n % 2 else s_va, (n - 4) // 2 + 1)
                tokens = dilated_tokens(max(s - 1, 0), t)
                for kk in range(KD):
                    rhs = wva[:, kk, :] if s == 0 else wvd[:, s - 1, kk, :]
                    mm = pe.matmul(k.psum[:, 4 + n % 4, 0:rhs.shape[-1]], tokens(hT[:, kk, :]), rhs,
                                   start=(kk == 0), stop=(kk == KD - 1))
                mm.then_inc(s_v, 1)


def stage_compress(k, w1c, w2c, s_cw, kc, vc):
    nc = k.nc
    with ExitStack() as mem:
        k.stage = mem
        sb = lambda n, s, d=F32: k.sbuf(mem, "c_" + n, s, d)
        kT2 = sb("kT2", [P, 2, NSA_KV, S])
        blk = sb("blk", [P, 2, LP, NSA_KV * NC])
        act1 = sb("gelu", [P, 2, 2, NSA_KV * NC])
        s_k = [k.sem(f"c_k{i}") for i in range(2)]
        s_zero, s_blk0, s_blk1, s_h, s_gelu, s_o, s_out = (k.sem("c_" + n) for n in (
            "zero", "blk_k", "blk_v", "hidden", "gelu", "out_ps", "out"))
        block = k.block(mem)

        @block.sync
        def _(sp):
            for kv in range(2):
                src = k.d_qk[R_CK + P * kv:R_CK + P * (kv + 1), :].rearrange("(h d) t -> d h t", d=DH)
                sp.dma_start(kT2[0:DH, kv], src).then_inc(s_k[kv], 16)
                sp.dma_start(kT2[DH:P, kv, :, 0:S - 1], src[:, :, 1:S]).then_inc(s_k[kv], 16)

        def blocks(eng, kv, done):
            eng.wait_ge(s_k[kv], 32)
            for lp in range(LP):
                src = kT2[:, kv, :, 2 * lp:2 * lp + CMP_STRIDE * (NC - 1) + 1:CMP_STRIDE]
                dst = blk[:, kv, lp, :].rearrange("p (h c) -> p h c", h=NSA_KV)
                col = 72 + LP * kv + lp
                eng.tensor_scalar(dst, src, k.vecT[:, col:col + 1], None, ALU.add).then_inc(done, 1)

        @block.gpsimd
        def _(pool):
            pool.memset(kc[:, :, :], 0.0).then_inc(s_zero, 1)
            pool.memset(vc[:, :, :], 0.0).then_inc(s_zero, 1)
            blocks(pool, 1, s_blk1)

        @block.vector
        def _(dve):
            blocks(dve, 0, s_blk0)
            dve.wait_ge(s_zero, 2)
            dve.wait_ge(s_o, 1)
            for x in range(2):
                dve.tensor_copy(kc[DH * x:DH * (x + 1), x, :], k.psum[0:DH, 4, 0:NSA_KV * NC]).then_inc(s_out, 1)
            dve.wait_ge(s_o, 2)
            dve.tensor_copy(vc[0:NC, :, :], k.psum[0:NC, 5, 0:NSA_KV * DH].rearrange("p (h d) -> p h d", d=DH)
                            ).then_inc(s_out, 1)

        @block.scalar
        def _(act):
            for kv in range(2):
                for hc in range(2):
                    act.wait_ge(s_h, 2 * kv + hc + 1)
                    act.activation(act1[:, kv, hc, :], k.psum[:, 2 * kv + hc, 0:NSA_KV * NC], ACT.Gelu_apprx_tanh
                                   ).then_inc(s_gelu, 1)

        @block.tensor
        def _(pe):
            pe.wait_ge(s_cw, 64)
            for kv in range(2):
                pe.wait_ge(s_blk1 if kv else s_blk0, LP)
                for hc in range(2):
                    for lp in range(LP):
                        mm = pe.matmul(k.psum[:, 2 * kv + hc, 0:NSA_KV * NC], w1c[:, kv, lp, hc * P:(hc + 1) * P],
                                       blk[:, kv, lp, :], start=(lp == 0), stop=(lp == LP - 1))
                    mm.then_inc(s_h, 1)
            pe.wait_ge(s_gelu, 2)
            for hc in range(2):
                mm = pe.matmul(k.psum[0:DH, 4, 0:NSA_KV * NC], w2c[:, 0, hc, :], act1[:, 0, hc, :],
                               start=(hc == 0), stop=(hc == 1))
            mm.then_inc(s_o, 1)
            pe.wait_ge(s_gelu, 4)
            for h in range(NSA_KV):
                for hc in range(2):
                    mm = pe.matmul(k.psum[0:NC, 5, h * DH:(h + 1) * DH], act1[:, 1, hc, h * NC:(h + 1) * NC],
                                   w2c[:, 1, hc, :], start=(hc == 0), stop=(hc == 1))
            mm.then_inc(s_o, 1)


LAG_T, LAG_V = 3, 5
RING = 8
BR = 8
SB_COLS = 1152


class Job:

    def __init__(self, q, keys, width, bias, values, small=False):
        self.q, self.keys, self.width, self.bias, self.small = q, keys, width, bias, small
        n = len(values)
        cut = n if n <= 4 else (n + 1) // 2
        self.chunks = [values[:cut]] + ([values[cut:]] if n > cut else [])


def attention(k, mem, name, count, jobs, ready, loads, finish, finish_pool, finish_sp, act_first=None):
    nc = k.nc
    sb = lambda n, s, d=F32: k.sbuf(mem, f"{name}_{n}", s, d)
    probs = [sb(f"probs{i}", [P, S]) for i in range(4)]
    pcmp = [sb(f"pcmp{i}", [P, P]) for i in range(4)]
    turned = [sb(f"turned{i}", [P, BANK]) for i in range(RING)]
    nmax = sb("nmax", [P, 8 * BR])
    den = sb("den", [P, 8 * BR])
    s_passed = k.sem(name + "_passed")
    s_scores, s_biased, s_probs, s_turned, s_even, s_odd, s_summed, s_branch, s_clear = (
        k.sem(f"{name}_{n}") for n in ("scores", "biased", "probs", "turned", "even", "odd", "summed", "branch",
                                       "clear"))
    sems = dict(scores=s_scores, biased=s_biased, branch=s_branch)
    block = k.block(mem)
    proto = jobs(0)
    nj = len(proto)
    nb = nj // BR
    chunk_of = []
    for j, job in enumerate(proto):
        chunk_of += [(j, n) for n in range(len(job.chunks))]
    nchunk = len(chunk_of)
    assert nchunk % RING == 0 and nj % 4 == 0 and nb % 2 == 0
    chunks_of = [[c for c, (j, _) in enumerate(chunk_of) if j == job] for job in range(nj)]
    last_chunk = [chunks_of[j][-1] for j in range(nj)]

    def at(i, n, idx):
        return i * n + (n + idx + 1)

    def tile(j):
        return (pcmp if proto[j].small else probs)[j % 4]

    @block.gpsimd
    def _(pool):
        for n, t in enumerate(pcmp):
            pool.memset(t[:, :], 0.0).then_inc(s_clear, 1)
            pool.wait_ge(s_clear, n + 1)
        ready["pool"](pool, s_branch, nb)
        with pool.Fori(0, count) as i:
            finish_pool(pool, i, at, nb, s_branch)
        ready["pool_end"](pool)

    @block.sync
    def _(sp):
        ready["sp"](sp)
        with sp.Fori(0, count) as i:
            loads(sp, i, at, sems, nj)
            finish_sp(sp, i, at, nb)
        ready["sp_end"](sp)

    @block.tensor
    def _(pe):
        pe.sem_inc(s_scores, nj)
        pe.sem_inc(s_turned, nchunk)
        pe.sem_inc(s_summed, nchunk)
        ready["pe"](pe)
        with pe.Fori(0, count) as i:
            js = jobs(i)
            for s in range(nj + LAG_V):
                if s < nj:
                    job = js[s]
                    ready["job"](pe, i, s)
                    pe.wait_ge(s_biased, at(i, nj, s - 2))
                    for rhs, col in job.keys:
                        bank = 2 * (s % 2) + col // BANK
                        mm = pe.matmul(k.psum[:, bank, 0:rhs.shape[-1]], job.q, rhs, start=True, stop=True)
                    mm.then_inc(s_scores, 1)
                j = s - LAG_T
                if 0 <= j < nj:
                    pe.wait_ge(s_probs, at(i, nj, j))
                    for n, c in enumerate(chunks_of[j]):
                        p = c - 2
                        pe.wait_ge(s_odd if c % 2 else s_even, at(i, nchunk // 2, p // 2))
                        first = 0 if n == 0 else len(js[j].chunks[0])
                        for q in range(len(js[j].chunks[n])):
                            col = (first + q) * P
                            mm = pe.transpose(k.psum[:, 4 + c % 2, q * P:(q + 1) * P], tile(j)[:, col:col + P],
                                              k.ident)
                        mm.then_inc(s_turned, 1)
                j = s - LAG_V
                if 0 <= j < nj:
                    br = j // BR
                    if j % BR == 0:
                        pe.wait_ge(s_branch, at(i, nb, br - 2))
                    total = sum(len(c) for c in js[j].chunks)
                    done = 0
                    for n, c in enumerate(chunks_of[j]):
                        pe.wait_ge(s_odd if c % 2 else s_even, at(i, nchunk // 2, c // 2))
                        for q, v in enumerate(js[j].chunks[n]):
                            o = (j % BR) * DH
                            mm = pe.matmul(k.psum[:, 6 + br % 2, o:o + DH], turned[c % RING][:, q * P:(q + 1) * P], v,
                                           start=(done == 0), stop=(done == total - 1))
                            done += 1
                        mm.then_inc(s_summed, 1)

    def copy_out(eng, i, c, sem):
        n = len(proto[chunk_of[c][0]].chunks[chunk_of[c][1]])
        eng.wait_ge(s_turned, at(i, nchunk, c))
        eng.wait_ge(s_summed, at(i, nchunk, c - RING))
        src = k.psum[:, 4 + c % 2, 0:n * P]
        dst = turned[c % RING][:, 0:n * P]
        (eng.copy(dst, src) if sem is s_even else eng.tensor_copy(dst, src)).then_inc(sem, 1)

    @block.scalar
    def _(act):
        act.sem_inc(s_probs, nj)
        act.sem_inc(s_even, nchunk // 2)
        with act.Fori(0, count) as i:
            js = jobs(i)
            act.wait_ge(s_branch, at(i, nb, -1))
            for s in range(nj + LAG_T):
                if s < nj:
                    w = js[s].width
                    act.wait_ge(s_biased, at(i, nj, s))
                    act.activation(tile(s)[:, 0:w], tile(s)[:, 0:w], ACT.Exp, scale=-1.0, bias=nmax[:, s:s + 1],
                                   accum_out=den[:, s:s + 1]).then_inc(s_probs, 1)
                j = s - LAG_T
                if 0 <= j < nj:
                    for c in chunks_of[j]:
                        if c % 2 == 0:
                            copy_out(act, i, c, s_even)

    @block.vector
    def _(dve):
        dve.sem_inc(s_biased, nj)
        dve.sem_inc(s_odd, nchunk // 2)
        dve.sem_inc(s_branch, nb)
        dve.wait_ge(s_clear, len(pcmp))
        with dve.Fori(0, count) as i:
            js = jobs(i)
            for s in range(nj + LAG_V + 1):
                if s < nj:
                    w = js[s].width
                    ready["bias"](dve, i, s)
                    dve.wait_ge(s_scores, at(i, nj, s))
                    prev = [c for c in chunks_of[s - 4]] if s >= 4 else [c - nchunk for c in chunks_of[nj + s - 4]]
                    dve.wait_ge(s_turned, at(i, nchunk, prev[-1]))
                    settle(dve, s_passed)
                    b = 2 * (s % 2)
                    src = k.psum[:, b:b + 2, :].rearrange("p a b -> p (a b)")[:, 0:w]
                    dve.tensor_tensor_reduce(tile(s)[:, 0:w], src, js[s].bias, -1.0, FLOOR, ALU.add, ALU.min,
                                             nmax[:, s:s + 1]).then_inc(s_biased, 1)
                j = s - LAG_T
                if 0 <= j < nj:
                    for c in chunks_of[j]:
                        if c % 2:
                            copy_out(dve, i, c, s_odd)
                j = s - LAG_V - 1
                if j >= 0 and j % BR == BR - 1:
                    br = j // BR
                    dve.wait_ge(s_summed, at(i, nchunk, last_chunk[j]))
                    dve.wait_ge(s_probs, at(i, nj, j))
                    out = k.psum[:, 6 + br % 2, :].rearrange("p (t d) -> p t d", d=DH)
                    cols = slice(br * BR, (br + 1) * BR)
                    finish(dve, i, at, br, nb, out, nmax[:, cols], den[:, cols], s_branch)


def stage_nsa(k, vA, gates, kc, vc, o_nsa):
    assert S // 64 <= 16
    nc = k.nc
    with ExitStack() as mem:
        k.stage = mem
        sb = lambda n, s, d=F32: k.sbuf(mem, "d_" + n, s, d)
        q = sb("q", [P, S])
        keys = sb("keys", [P, 2, NSA_KV, 2, S])
        b_sel = [sb(f"b_sel{x}", [P, S]) for x in range(2)]
        b_win = [sb(f"b_win{x}", [P, WIN_TILES * P]) for x in range(2)]
        b_cmp = [sb(f"b_cmp{x}", [P, 120]) for x in range(2)]
        tmp = [sb(f"tmp{i}", [P, NT, DH]) for i in range(2)]
        small = sb("small", [P, 6, 3, BR])
        s_keys, s_zero, s_q, s_acc, s_small = (k.sem("d_" + n) for n in (
            "keys", "zero", "q", "acc", "small"))
        s_b = [k.sem(f"d_bias{x}") for x in range(2)]
        s_pool_passed, s_clear, s_fill = k.sem("d_pool_passed"), k.sem("d_zeroed"), k.sem("d_fill")
        zero = sb("zero", [P, BANK])

        def jobs(i):
            kv = i // 2
            out = []
            for x in range(2):
                for t in reversed(range(NT)):
                    n = t + 1
                    out.append(Job(q[:, t * P:n * P],
                                   [(keys[:, 0, bass.ds(kv, 1), x, c:min(c + BANK, n * P)].rearrange("p a b -> p (a b)"), c)
                                    for c in range(0, n * P, BANK)], n * P, b_sel[x][:, S - n * P:S],
                                   [vA[:, kt, bass.ds(kv * DH, DH)] for kt in range(n)]))
                for t in reversed(range(NT)):
                    lo = max(0, t - WIN_TILES + 1)
                    n = t + 1 - lo
                    out.append(Job(q[:, t * P:(t + 1) * P],
                                   [(keys[:, 1, bass.ds(kv, 1), x, lo * P + c:lo * P + min(c + BANK, n * P)]
                                     .rearrange("p a b -> p (a b)"), c)
                                    for c in range(0, n * P, BANK)], n * P, b_win[x][:, (WIN_TILES - n) * P:],
                                   [vA[:, kt, bass.ds(kv * DH + P, DH)] for kt in range(lo, t + 1)]))
                for t in reversed(range(NT)):
                    c0 = 8 * (NT - 1 - t)
                    out.append(Job(q[:, t * P:(t + 1) * P], [(kc[:, x, bass.ds(kv * NC, NC)], 0)], NC,
                                   b_cmp[x][:, c0:c0 + NC], [vc[:, bass.ds(kv, 1), :].rearrange("p a b -> p (a b)")],
                                   small=True))
            return out

        def sp_ready(sp):
            for br, row in ((0, R_SK), (1, R_WK)):
                for x in range(2):
                    sp.dma_start(keys[DH * x:DH * (x + 1), br, :, x, :],
                                 k.d_qk[row:row + P, :].rearrange("(h d) t -> d h t", d=DH)).then_inc(s_keys, 16)

        def pool_ready(pool):
            for br in range(2):
                for x in range(2):
                    pool.memset(keys[DH * (1 - x):DH * (2 - x), br, :, x, :], 0.0).then_inc(s_zero, 1)
                    pool.wait_ge(s_zero, 2 * br + x + 1)

        def pe_ready(pe):
            pe.wait_ge(s_keys, 64)
            pe.wait_ge(s_zero, 4)

        def loads(sp, i, at, sems, nj):
            sp.wait_ge(sems["scores"], at(i, nj, -1))
            sp.dma_start(q[:, :], k.d_qk[bass.ds(i * P, P), :]).then_inc(s_q, 16)
            for x in range(2):
                sp.wait_ge(sems["biased"], at(i, nj, (x + 1) * (nj // 2) - 1 - nj))
                h = i * 2 + x
                for dst, src, w in ((b_sel, k.d_sel, S), (b_win, k.d_win, WIN_TILES * P), (b_cmp, k.d_cmp, 119)):
                    sp.dma_start(dst[x][:, 0:w], src[bass.ds(h, 1)].rearrange("h p w -> (h p) w")[:, 0:w]
                                 ).then_inc(s_b[x], 16)

        def job_ready(pe, i, s):
            if s == 0:
                pe.wait_ge(s_q, 16 * i + 16)

        def bias_ready(dve, i, s):
            if s % 24 == 0:
                dve.wait_ge(s_b[s // 24], 48 * i + 48)

        def finish(dve, i, at, br, nb, out, nmax, den, s_branch):
            x, kind = divmod(br, 3)
            gate = gates[:, :, bass.ds(i * 2 + (8 * ((kind + 1) % 3) + x), 1)].rearrange("p t a -> p (t a)")
            nonzero, inv, coef = small[:, br, 0, :], small[:, br, 1, :], small[:, br, 2, :]
            base = i * 18 + 3 * br
            dve.tensor_scalar(nonzero, den, 0.5, None, ALU.max).then_inc(s_small, 1)
            dve.wait_ge(s_small, base + 1)
            dve.reciprocal(inv, nonzero).then_inc(s_small, 1)
            dve.wait_ge(s_small, base + 2)
            dve.tensor_tensor(coef, inv[:, ::-1], gate, ALU.mult).then_inc(s_small, 1)
            dve.wait_ge(s_small, base + 3)
            wide = coef.unsqueeze(2).to_broadcast([P, BR, DH])
            out = out[:, ::-1, :]
            h0 = i * (2 * DH) + x * DH
            if kind == 0:
                dve.tensor_tensor(o_nsa[:, :, bass.ds(h0, DH)], out, wide, ALU.mult).then_inc(s_branch, 1)
            else:
                dve.wait_ge(s_acc, i * 4 + (2 * x + kind + 1))
                dve.tensor_tensor(tmp[kind - 1][:, :, :], out, wide, ALU.mult).then_inc(s_branch, 1)

        def finish_pool(pool, i, at, nb, s_branch):
            for br in (1, 2, 4, 5):
                x, kind = divmod(br, 3)
                pool.wait_ge(s_branch, at(i, nb, br))
                if kind == 2:
                    pool.wait_ge(s_acc, i * 4 + (2 * x + 3))
                settle(pool, s_pool_passed)
                h0 = i * (2 * DH) + x * DH
                dst = o_nsa[:, :, bass.ds(h0, DH)]
                pool.tensor_tensor(dst, dst, tmp[kind - 1][:, :, :], ALU.add).then_inc(s_acc, 1)

        def pool_start(pool, s_branch, nb):
            pool_ready(pool)
            pool.sem_inc(s_acc, 2)
            pool.memset(zero[:, :], 0.0).then_inc(s_clear, 1)
            pool.wait_ge(s_clear, 1)
            pool.wait_ge(s_branch, nb + 1)
            first = 2 * S // P
            pool.dma_start(k.d_y[first * P:, :].rearrange("(p b) (h d) -> p (b h) d", p=P, d=BANK),
                           zero[:, :].unsqueeze(1).to_broadcast([P, (MAXBLK - first) * D // BANK, BANK])).then_inc(s_fill, 16)

        attention(k, mem, "nsa", NSA_H // 2, jobs,
                  dict(sp=sp_ready, sp_end=lambda sp: None, pool=pool_start, pool_end=lambda pool: pool.wait_ge(s_fill, 16), pe=pe_ready, job=job_ready,
                       bias=bias_ready), loads, finish, finish_pool, lambda *a: None)


def stage_dilated(k, vD):
    nc = k.nc
    with ExitStack() as mem:
        k.stage = mem
        sb = lambda n, s, d=F32: k.sbuf(mem, "e_" + n, s, d)
        q = [sb(f"q{g}", [P, S]) for g in range(DIL_G)]
        keys = [sb(f"keys{g}", [P, 2, S]) for g in range(DIL_G)]
        bias = [sb(f"bias{g}", [P, 2, 2 * P]) for g in range(DIL_G)]
        stage = [sb(f"stage{i}", [P, NT, DH + 2]) for i in range(2)]
        s_zero = k.sem("e_zero")
        s_in = [k.sem(f"e_in{g}") for g in range(DIL_G)]
        s_store = [k.sem(f"e_store{i}") for i in range(2)]
        s_cp, s_staged = k.sem("e_copied"), k.sem("e_staged")

        def jobs(i):
            out = []
            for g in range(DIL_G):
                for x in range(2):
                    for slot in range(NT):
                        qs = dilated_tokens(g, slot)(q[g])
                        v = lambda t: vD[:, g, t, bass.ds(i * P + x * DH, DH)]
                        two = g == 0 and slot > 0 or g == 1 and slot % 2 == 1
                        if g == 0:
                            ks = keys[g][:, x, (slot - two) * P:(slot + 1) * P]
                        elif g == 1:
                            r = slot // 2
                            ks = keys[g][:, x, r:r + (S if two else S // 2) - 3:4]
                        else:
                            ks = dilated_tokens(g, slot)(keys[g][:, x, :])
                        b = bias[g][:, x, P - two * P:2 * P] if g < 2 else bias[g][:, x, 0:P]
                        out.append(Job(qs, [(ks, 0)], P * (1 + two), b, [v(slot - 1), v(slot)] if two else [v(slot)]))
            return out

        def pool_ready(pool, s_branch, nb):
            for g in range(DIL_G):
                for x in range(2):
                    pool.memset(keys[g][DH * (1 - x):DH * (2 - x), x, :], 0.0).then_inc(s_zero, 1)
                    pool.wait_ge(s_zero, 2 * g + x + 1)

        def loads(sp, i, at, sems, nj):
            for g in range(DIL_G):
                sp.wait_ge(sems["scores"], at(i, nj, (g + 1) * 2 * BR - 1 - nj))
                sp.wait_ge(sems["biased"], at(i, nj, (g + 1) * 2 * BR - 1 - nj))
                r = DIL_H * DH * g
                sp.dma_start(q[g][:, :], k.d_qk[bass.ds(i * P + (R_DQ + r), P), :]).then_inc(s_in[g], 16)
                for x in range(2):
                    sp.dma_start(keys[g][DH * x:DH * (x + 1), x, :],
                                 k.d_qk[bass.ds(i * P + (R_DK + r + DH * x), DH), :]).then_inc(s_in[g], 16)
                    w = 2 * P if g < 2 else P
                    sp.dma_start(bias[g][:, x, 0:w], k.d_dtab[g, bass.ds(i * 2 + x, 1)].rearrange(
                        "h p w -> (h p) w")[:, 0:w]).then_inc(s_in[g], 16)

        def job_ready(eng, i, s):
            if s % (2 * BR) == 0:
                eng.wait_ge(s_in[s // (2 * BR)], 80 * i + 80)

        def finish(dve, i, at, br, nb, out, nmax, den, s_branch):
            st = stage[br % 2]
            dve.wait_ge(s_store[br % 2], store_value(i, br - 2))
            dve.tensor_copy(st[:, :, DH], nmax).then_inc(s_cp, 1)
            dve.tensor_copy(st[:, :, DH + 1], den).then_inc(s_cp, 1)
            dve.tensor_copy(st[:, :, 0:DH], out).then_inc(s_branch, 1)
            dve.wait_ge(s_cp, i * 12 + (2 * br + 2))
            dve.wait_ge(s_branch, at(i, nb, br))
            dve.sem_inc(s_staged, 1)

        def store_value(i, br):
            n = 3 * i + (br // 2 + 4)
            return n * 32

        def finish_sp(sp, i, at, nb):
            for br in range(nb):
                g, x = divmod(br, 2)
                st = stage[br % 2]
                sp.wait_ge(s_staged, i * 6 + (br + 1))
                head = i * 2 + x
                rows = k.d_dil[g, :, bass.ds(head, 1), :]
                for half in range(2):
                    if g == 0:
                        dst = rows.rearrange("(t p) h c -> p t (h c)", p=P)[:, 4 * half:4 * half + 4, :]
                        src = st[:, 4 * half:4 * half + 4, :]
                    elif g == 1:
                        dst = rows.rearrange("(b j r) h c -> b j r (h c)", b=2, r=4)[half]
                        src = st[:, half::2, :]
                    else:
                        dst = rows.rearrange("(m w) h c -> m w (h c)", w=8)[:, 4 * half:4 * half + 4, :]
                        src = st[:, 4 * half:4 * half + 4, :]
                    sp.dma_start(dst, src).then_inc(s_store[br % 2], 16)

        def sp_ready(sp):
            for i in range(2):
                sp.sem_inc(s_store[i], 96)

        def sp_end(sp):
            for i in range(2):
                sp.wait_ge(s_store[i], 96 * 3)

        attention(k, mem, "dil", DIL_H // 2, jobs,
                  dict(sp=sp_ready, sp_end=sp_end, pool=pool_ready, pool_end=lambda pool: None, pe=lambda pe: pe.wait_ge(s_zero, 6),
                       job=job_ready, bias=job_ready),
                  loads, finish, lambda *a: None, finish_sp)


def stage_join(k, o_nsa, oT):
    nc = k.nc
    with ExitStack() as mem:
        k.stage = mem
        sb = lambda n, s, d=F32: k.sbuf(mem, "f_" + n, s, d)
        dl = sb("dl", [P, DIL_G, NT, DIL_H, DH + 2])
        mn = sb("mn", [P, NT, DIL_H])
        w, wd = sb("w", [P, DIL_G, NT, DIL_H]), sb("wd", [P, DIL_G, NT, DIL_H])
        tot, tot2, inv = (sb(n, [P, NT, DIL_H]) for n in ("tot", "tot2", "inv"))
        part = [sb(f"part{g}", [P, NT, DIL_H, DH]) for g in range(DIL_G)]
        s_dl, s_v, s_w, s_part1, s_sum, s_tr, s_eva, s_evd = (k.sem("f_" + n) for n in (
            "dl", "dve", "weights", "part1", "sum", "transposed", "evac_act", "evac_dve"))
        o_dil = part[0]
        block = k.block(mem)
        groups = [(c, tg) for c in range(6) for tg in range(2)]

        @block.sync
        def _(sp):
            for g in range(DIL_G):
                sp.dma_start(dl[:, g].rearrange("p t h c -> p t (h c)"),
                             k.d_dil[g].rearrange("(t p) h c -> p t (h c)", p=P)).then_inc(s_dl, 16)

        @block.vector
        def _(dve):
            v = Count(s_v)
            dve.wait_ge(s_dl, 48)
            nm = lambda g: dl[:, g, :, :, DH]
            v.inc(dve.tensor_tensor(mn[:, :, :], nm(0), nm(1), ALU.min))
            v.wait(dve)
            v.inc(dve.tensor_tensor(mn[:, :, :], mn[:, :, :], nm(2), ALU.min))
            v.wait(dve)
            for g in range(DIL_G):
                v.inc(dve.tensor_tensor(w[:, g], mn[:, :, :], nm(g), ALU.subtract))
            dve.wait_ge(s_w, 1)
            for g in range(DIL_G):
                v.inc(dve.tensor_tensor(wd[:, g], w[:, g], dl[:, g, :, :, DH + 1], ALU.mult))
            v.wait(dve)
            v.inc(dve.tensor_tensor(tot[:, :, :], wd[:, 0], wd[:, 1], ALU.add))
            v.wait(dve)
            v.inc(dve.tensor_tensor(tot2[:, :, :], tot[:, :, :], wd[:, 2], ALU.add))
            v.wait(dve)
            v.inc(dve.reciprocal(inv[:, :, :], tot2[:, :, :]))
            v.wait(dve)
            for g in range(DIL_G):
                v.inc(dve.tensor_tensor(w[:, g], w[:, g], inv[:, :, :], ALU.mult))
            v.wait(dve)
            for g in (0, 2):
                wide = w[:, g].unsqueeze(3).to_broadcast([P, NT, DIL_H, DH])
                v.inc(dve.tensor_tensor(part[g][:, :, :, :], dl[:, g, :, :, 0:DH], wide, ALU.mult))
            v.wait(dve)
            v.inc(dve.tensor_tensor(part[0][:, :, :, :], part[0][:, :, :, :], part[2][:, :, :, :], ALU.add))
            v.wait(dve)
            dve.wait_ge(s_part1, 1)
            dve.tensor_tensor(o_dil[:, :, :, :], part[0][:, :, :, :], part[1][:, :, :, :], ALU.add).then_inc(s_sum, 1)
            for n, (c, tg) in enumerate(groups):
                if n % 2 and c >= 4:
                    dve.wait_ge(s_tr, n + 1)
                    dve.tensor_copy(oT[:, c, tg * BANK:(tg + 1) * BANK], k.psum[:, n % 4, :]).then_inc(s_evd, 1)

        @block.gpsimd
        def _(pool):
            pool.wait_ge(s_v, 15)
            wide = w[:, 1].unsqueeze(3).to_broadcast([P, NT, DIL_H, DH])
            pool.tensor_tensor(part[1][:, :, :, :], dl[:, 1, :, :, 0:DH], wide, ALU.mult).then_inc(s_part1, 1)

        @block.scalar
        def _(act):
            act.wait_ge(s_v, 5)
            act.activation(w[:, :, :, :], w[:, :, :, :], ACT.Exp).then_inc(s_w, 1)
            for n, (c, tg) in enumerate(groups):
                if n % 2 == 0 or c < 4:
                    act.wait_ge(s_tr, n + 1)
                    act.copy(oT[:, c, tg * BANK:(tg + 1) * BANK], k.psum[:, n % 4, :]).then_inc(s_eva, 1)

        @block.tensor
        def _(pe):
            for n, (c, tg) in enumerate(groups):
                if n == 8:
                    pe.wait_ge(s_sum, 1)
                if n >= 4:
                    pe.wait_ge(s_eva, n - 3)
                for q in range(4):
                    t = 4 * tg + q
                    src = o_nsa[:, t, c * P:(c + 1) * P] if c < 4 else \
                        o_dil[:, t].rearrange("p h d -> p (h d)")[:, (c - 4) * P:(c - 3) * P]
                    mm = pe.transpose(k.psum[:, n % 4, q * P:(q + 1) * P], src, k.ident)
                mm.then_inc(s_tr, 1)


def stage_merge(k, hT, oT, mT, acc, g1row, g2row, w_o, s_wo):
    nc = k.nc
    with ExitStack() as mem:
        k.stage = mem
        sb = lambda n, s, d=F32: k.sbuf(mem, "g_" + n, s, d)
        wn = [sb(f"wn{i}", [P, 4, P]) for i in range(2)]
        wd = [sb(f"wd{i}", [P, 2, P]) for i in range(2)]
        wm = [sb(f"wm{i}", [P, 2, KD, P]) for i in range(2)]
        ada = sb("ada", [P, 1, KD, BANK])
        sg = [sb(f"sg{i}", [P, 2, BANK]) for i in range(2)]
        tt = [sb(f"tt{i}", [P, 2, BANK]) for i in range(2)]
        s_w = [k.sem(f"g_w{i}") for i in range(2)]
        s_ada = [k.sem(f"g_ada{i}") for i in range(2)]
        s_passed, s_gb, s_accp = k.sem("g_pool_passed"), k.sem("g_ada_b"), k.sem("g_dve_passed")
        s_gate, s_up, s_acc, s_sig, s_mul, s_sum, s_bc, s_bcc, s_col, s_mod = (k.sem("g_" + n) for n in (
            "gates_ps", "ups_ps", "acc", "sigmoids", "products", "merged", "bcast_ps", "bcast",
            "cols_ps", "mod"))
        w_in = k.w_in[0].rearrange("(k p) n -> p k n", p=P)
        ada_w = k.ada_w[0].rearrange("(k p) n -> p k n", p=P)
        block = k.block(mem)

        @block.sync
        def _(sp):
            for row, c in ((g1row, 2 * D), (g2row, 5 * D)):
                sp.dma_start(row[:, :], k.ada_b[:, c:c + D].partition_broadcast(P).rearrange("p a n -> p (a n)")
                             ).then_inc(s_gb, 16)
            with sp.Fori(0, KD // 2) as i:
                for s in range(2):
                    sp.wait_ge(s_up, 4 * i + (2 * s + 2))
                    c = i * (2 * P) + s * P
                    sp.dma_start(wm[s][:, 0], w_in[:, :, bass.ds(c + C_MERGE, P)]).then_inc(s_w[s], 16)
                    sp.dma_start(wm[s][:, 1], w_in[:, :, bass.ds(c + (C_MERGE + D), P)]).then_inc(s_w[s], 16)
                    sp.dma_start(wn[s][:, :, :], k.w_up_nsa[0].rearrange("(k p) n -> p k n", p=P)[:, :, bass.ds(c, P)]
                                 ).then_inc(s_w[s], 16)
                    sp.dma_start(wd[s][:, :, :], k.w_up_dil[0].rearrange("(k p) n -> p k n", p=P)[:, :, bass.ds(c, P)]
                                 ).then_inc(s_w[s], 16)
                    sp.wait_ge(s_acc, 2 * KD * i + KD * (s + 1))
                    sp.dma_start(ada[:, 0], ada_w[:, :, bass.ds(i * (2 * BANK) + (4 + s) * BANK, BANK)]
                                 ).then_inc(s_ada[s], 16)
            sp.dma_start(w_o[:, :, :], k.w_o[0].rearrange("(k p) n -> p k n", p=P)).then_inc(s_wo, 16)

        @block.scalar
        def _(act):
            act.sem_inc(s_sig, 4)
            with act.Fori(0, KD // 2) as i:
                for u in range(4):
                    act.wait_ge(s_gate, 4 * i + (u + 5))
                    act.wait_ge(s_mul, 4 * i + (u + 3))
                    src = k.psum[:, 2 * (u % 2):2 * (u % 2) + 2, :]
                    act.activation(sg[u % 2][:, :, :], src, ACT.Sigmoid).then_inc(s_sig, 1)

        @block.vector
        def _(dve):
            dve.sem_inc(s_mul, 4)
            dve.sem_inc(s_acc, KD)
            with dve.Fori(0, KD // 2) as i:
                for u in range(4):
                    dve.wait_ge(s_sig, 4 * i + (u + 5))
                    dve.wait_ge(s_up, 4 * i + (u + 5))
                    dve.wait_ge(s_sum, 4 * i + (u + 3))
                    dve.tensor_tensor(tt[u % 2][:, :, :], k.psum[:, 4:6, :], sg[u % 2][:, :, :], ALU.mult
                                      ).then_inc(s_mul, 1)
                    if u % 2:
                        s = u // 2
                        dve.wait_ge(s_ada[s], 16 * i + 16)
                        mod_products(dve, k, ada, 0, acc[:, bass.ds(i * (2 * BANK) + s * BANK, BANK)], s_acc,
                                     2 * KD * i + KD * (s + 1), s_accp)
            dve.wait_ge(s_col, 1)
            dve.tensor_tensor(k.mod[:, 16:48], k.psum[:, 7, 0:32], k.vecT[:, 40:72], ALU.add).then_inc(s_mod, 1)
            dve.wait_ge(s_mod, 1)
            dve.scalar_tensor_tensor(k.modA[:, 1, :], k.mod[:, 32:40], 1.0, k.vecT[:, 16:24], ALU.add, ALU.mult
                                     ).then_inc(s_mod, 1)
            dve.wait_ge(s_gb, 32)
            for n in range(4):
                dve.wait_ge(s_bc, n + 1)
                dst = (g1row if n < 2 else g2row)[:, (n % 2) * BANK:(n % 2 + 1) * BANK]
                dve.tensor_tensor(dst, k.psum[:, n, :], dst, ALU.add).then_inc(s_bcc, 1)

        @block.gpsimd
        def _(pool):
            pool.sem_inc(s_sum, 4)
            with pool.Fori(0, KD // 2) as i:
                for u in range(4):
                    pool.wait_ge(s_mul, 4 * i + (u + 5))
                    settle(pool, s_passed)
                    s, half = divmod(u, 2)
                    pool.tensor_tensor(mT[:, bass.ds(i * 2 + s, 1), half * BANK:(half + 1) * BANK]
                                       .rearrange("p a b -> p (a b)"),
                                       tt[half][:, 0, :], tt[half][:, 1, :], ALU.add).then_inc(s_sum, 1)

        @block.tensor
        def _(pe):
            pe.sem_inc(s_gate, 4)
            pe.sem_inc(s_up, 4)
            with pe.Fori(0, KD // 2) as i:
                for u in range(4):
                    s, half = divmod(u, 2)
                    tok = slice(half * BANK, (half + 1) * BANK)
                    if half == 0:
                        pe.wait_ge(s_w[s], 64 * i + 64)
                    pe.wait_ge(s_sig, 4 * i + (u + 3))
                    for gate in range(2):
                        for kk in range(KD):
                            mm = pe.matmul(k.psum[:, 2 * half + gate, :], wm[s][:, gate, kk, :], hT[:, kk, tok],
                                           start=(kk == 0), stop=(kk == KD - 1))
                    mm.then_inc(s_gate, 1)
                    pe.wait_ge(s_mul, 4 * i + (u + 4))
                    for kk in range(4):
                        pe.matmul(k.psum[:, 4, :], wn[s][:, kk, :], oT[:, kk, tok], start=(kk == 0), stop=(kk == 3))
                    for kk in range(2):
                        mm = pe.matmul(k.psum[:, 5, :], wd[s][:, kk, :], oT[:, 4 + kk, tok],
                                       start=(kk == 0), stop=(kk == 1))
                    mm.then_inc(s_up, 1)
            pe.wait_ge(s_acc, KD * (KD + 1))
            mod_columns(pe, k, acc, 7, 32, s_col)
            ones = k.const[:, K_ONE:K_ONE + P]
            for n in range(4):
                c = (0 if n < 2 else 3 * D) + (n % 2) * BANK
                pe.matmul(k.psum[:, n, :], ones, acc[:, c:c + BANK], start=True, stop=True).then_inc(s_bc, 1)


def stage_out(k, mT, g1row, w_o, x2, logits, s_wo):
    nc = k.nc
    with ExitStack() as mem:
        k.stage = mem
        sb = lambda n, s, d=F32: k.sbuf(mem, "h_" + n, s, d)
        xn = [sb(f"xn{i}", [P, D]) for i in range(2)]
        h2T = [sb(f"h2T{i}", [P, KD, P]) for i in range(2)]
        tmp = sb("tmp", [P, 2, D])
        sq = sb("sq", [P, D])
        ss, var, std, rstd = (sb(n, [P, NT]) for n in ("ss", "var", "std", "rstd"))
        wr = sb("wr", [P, KD, NG + NE])
        rb = sb("rb", [P, NG + NE])
        (s_in, s_o, s_mul, s_x, s_ss, s_var, s_std, s_rstd, s_xn, s_tr, s_ha, s_hd, s_log, s_logc) = (
            k.sem("h_" + n) for n in ("in", "out_ps", "gated", "x2", "ss", "var", "std", "rstd", "xn",
                                      "transposed", "h_act", "h_dve", "logits_ps", "logits"))
        s_x2 = [k.sem(f"h_residual{i}") for i in range(4)]
        s_store = [k.sem(f"h_store{i}") for i in range(2)]
        block = k.block(mem)

        @block.sync
        def _(sp):
            for i in range(4):
                sp.dma_start(x2[:, 2 * i:2 * i + 2, :], k.x[0].rearrange("(t p) d -> p t d", p=P)[:, 2 * i:2 * i + 2]
                             ).then_inc(s_x2[i], 16)
            sp.dma_start(wr[:, :, 0:NG], k.router_wg[0].rearrange("(k p) n -> p k n", p=P)).then_inc(s_in, 16)
            sp.dma_start(wr[:, :, NG:], k.router_we[0].rearrange("(k p) n -> p k n", p=P)).then_inc(s_in, 16)
            sp.dma_start(rb[:, 0:NG], k.router_bg.partition_broadcast(P).rearrange("p a n -> p (a n)")).then_inc(s_in, 16)
            sp.dma_start(rb[:, NG:], k.router_be.partition_broadcast(P).rearrange("p a n -> p (a n)")).then_inc(s_in, 16)
            for t in range(NT):
                sp.wait_ge(s_xn, t + 1)
                sp.dma_start(k.d_xn[t * P:(t + 1) * P, :], xn[t % 2][:, :]).then_inc(s_store[t % 2], 16)
            for i in range(2):
                sp.wait_ge(s_store[i], 16 * (NT // 2))

        @block.tensor
        def _(pe):
            def turn(t):
                pe.wait_ge(s_xn, t + 1)
                if t >= 1:
                    pe.wait_ge(s_ha, 4 * t)
                    pe.wait_ge(s_hd, 4 * t)
                for kk in range(KD):
                    tr = pe.transpose(k.psum[:, 4 + kk // 4, (kk % 4) * P:(kk % 4 + 1) * P],
                                      xn[t % 2][:, kk * P:(kk + 1) * P], k.ident)
                    if kk % 4 == 3:
                        tr.then_inc(s_tr, 1)

            def route(t):
                pe.wait_ge(s_ha, 4 * t + 4)
                pe.wait_ge(s_hd, 4 * t + 4)
                if t == 0:
                    pe.wait_ge(s_in, 64)
                c = t * (NG + NE)
                for kk in range(KD):
                    mm = pe.matmul(k.psum[:, 6, c:c + NG + NE], h2T[t % 2][:, kk, :], wr[:, kk, :],
                                   start=(kk == 0), stop=(kk == KD - 1))
                mm.then_inc(s_log, 1)

            pe.wait_ge(s_wo, 16)
            for t in range(NT + 2):
                if t < NT:
                    if t >= 2:
                        pe.wait_ge(s_mul, t - 1)
                    for half in range(2):
                        for kk in range(KD):
                            mm = pe.matmul(k.psum[:, 2 * (t % 2) + half, :], mT[:, kk, t * P:(t + 1) * P],
                                           w_o[:, kk, half * BANK:(half + 1) * BANK],
                                           start=(kk == 0), stop=(kk == KD - 1))
                    mm.then_inc(s_o, 1)
                if 1 <= t <= NT:
                    turn(t - 1)
                if t >= 2:
                    route(t - 2)

        @block.vector
        def _(dve):
            for t in range(NT + 1):
                if t < NT:
                    dve.wait_ge(s_o, t + 1)
                    if t >= 2:
                        dve.wait_ge(s_x, t - 1)
                    b = 2 * (t % 2)
                    dve.tensor_tensor(tmp[:, t % 2, :], k.psum[:, b:b + 2, :].rearrange("p a b -> p (a b)"),
                                      g1row[:, :], ALU.mult).then_inc(s_mul, 1)
                    col = slice(t, t + 1)
                    dve.wait_ge(s_ss, t + 1)
                    dve.tensor_scalar(var[:, col], ss[:, col], 1.0 / D, EPS, ALU.mult, ALU.add).then_inc(s_var, 1)
                    dve.wait_ge(s_std, t + 1)
                    dve.reciprocal(rstd[:, col], std[:, col]).then_inc(s_rstd, 1)
                    dve.wait_ge(s_rstd, t + 1)
                    if t >= 2:
                        dve.wait_ge(s_store[t % 2], 16 * (t // 2))
                        dve.wait_ge(s_tr, 2 * (t - 1))
                    dve.tensor_scalar(xn[t % 2][:, :], x2[:, t, :], rstd[:, col], None, ALU.mult).then_inc(s_xn, 1)
                if t >= 1:
                    u = t - 1
                    dve.wait_ge(s_tr, 2 * u + 1)
                    if u >= 2:
                        dve.wait_ge(s_log, u - 1)
                    for kk in range(4):
                        dve.tensor_scalar(h2T[u % 2][:, kk, :], k.psum[:, 4, kk * P:(kk + 1) * P],
                                          k.modA[:, 1, kk:kk + 1], k.mod[:, 24 + kk:25 + kk], ALU.mult, ALU.add
                                          ).then_inc(s_hd, 1)
            dve.wait_ge(s_log, NT)
            dve.tensor_tensor(logits[:, :, :], k.psum[:, 6, 0:NT * (NG + NE)].rearrange("p (t e) -> p t e", t=NT),
                              rb[:, :].unsqueeze(1).to_broadcast([P, NT, NG + NE]), ALU.add).then_inc(s_logc, 1)

        @block.gpsimd
        def _(pool):
            for t in range(NT):
                if t % 2 == 0:
                    pool.wait_ge(s_x2[t // 2], 16)
                pool.wait_ge(s_mul, t + 1)
                pool.tensor_tensor(x2[:, t, :], x2[:, t, :], tmp[:, t % 2, :], ALU.add).then_inc(s_x, 1)

        @block.scalar
        def _(act):
            for t in range(NT + 1):
                if t < NT:
                    col = slice(t, t + 1)
                    act.wait_ge(s_x, t + 1)
                    if t >= 1:
                        act.wait_ge(s_ss, t)
                    act.activation(sq[:, :], x2[:, t, :], ACT.Square, accum_out=ss[:, col]).then_inc(s_ss, 1)
                    act.wait_ge(s_var, t + 1)
                    act.activation(std[:, col], var[:, col], ACT.Sqrt).then_inc(s_std, 1)
                if t >= 1:
                    u = t - 1
                    act.wait_ge(s_tr, 2 * u + 2)
                    if u >= 2:
                        act.wait_ge(s_log, u - 1)
                    for kk in range(4, KD):
                        act.activation(h2T[u % 2][:, kk, :], k.psum[:, 5, (kk - 4) * P:(kk - 3) * P], ACT.Identity,
                                       scale=k.modA[:, 1, kk:kk + 1], bias=k.mod[:, 24 + kk:25 + kk]).then_inc(s_ha, 1)


def stage_moe(k, x2, logits, g2row):
    nc = k.nc
    with ExitStack() as mem:
        k.stage = mem
        sb = lambda n, s, d=F32: k.sbuf(mem, "m_" + n, s, d)
        w1, w3 = ([sb(f"{n}{i}", [P, KD, DE]) for i in range(2)] for n in ("w1_", "w3_"))
        w2 = [sb(f"w2_{i}", [P, KE, D]) for i in range(2)]
        xg = [sb(f"xg{i}", [P, D]) for i in range(2)]
        xT = [sb(f"xT{i}", [P, KD, P]) for i in range(2)]
        sg = [sb(f"sg{i}", [P, DE]) for i in range(2)]
        hh = [sb(f"hh{i}", [P, DE]) for i in range(2)]
        hT = [sb(f"hT{i}", [P, KE, P]) for i in range(2)]
        ys_all, hots = sb("ys", [P, 2, D]), sb("one_hots", [P, 4, D])
        ys = [ys_all[:, i, :] for i in range(2)]
        spare = [w[:, 2 * q:2 * q + 2, :].rearrange("p a b -> p (a b)") for w in w1 + w3 for q in range(KD // 2)]
        ya, yb = spare[0::2], spare[1::2]
        nf = sb("nf", [P, D])
        idxs = [sb(f"idxs{i}", [P, 1], I32) for i in range(2)]
        dest_i = sb("dest_i", [P, 2, NT], I32)
        slot_i = sb("slot_i", [P, MAXBLK + 1], I32)
        be_i = sb("be_i", [1, MAXBLK], I32)
        nb_i = sb("nb_i", [1, 1], I32)
        wts = sb("wts", [P, 2, NT])
        ss, var, std, rstd = (sb(n, [P, NT]) for n in ("ss", "var", "std", "rstd"))
        gmax, se, pg, gm_, dv, ev, es, er = (sb(n, [P, NT]) for n in (
            "gmax", "se", "pg", "first", "dv", "ev", "es", "er"))
        dl, el, eq, cand, one, gmask = (sb(n, [P, NT, NG]) for n in ("dl", "el", "eq", "cand", "one", "gmask"))
        lem = sb("lem", [P, NT, NE])
        top = sb("top", [P, NT, 8])
        topi = sb("topi", [P, NT, 8], U32)
        ef = sb("ef", [P, NT, 2])
        hot = sb("hot", [P, 2, NT, NE])
        both = sb("both", [P, NT, NE])
        cnt, nb, end, start = (sb(n, [P, NE]) for n in ("cnt", "nb", "end", "start"))
        over = sb("over", [P, NE, NT])
        base = sb("base", [P, NT, NE])
        pick = sb("pick", [P, 2, NT, NE])
        dest, blkno, row = (sb(n, [P, 2, NT]) for n in ("dest", "blkno", "row"))
        rowhot = hots[:, 0:2, :].rearrange("p a (j r) -> p (a j) r", r=P)
        ge = hots[:, 2, 0:2 * NT * (MAXBLK + 1)].rearrange("p (j b) -> p j b", j=2 * NT)
        inblk = hots[:, 3, 0:2 * NT * MAXBLK].rearrange("p (j b) -> p j b", j=2 * NT)
        ended = ys_all[0:1, :, :].rearrange("p a b -> p (a b)")[:, 0:MAXBLK * NE].rearrange("p (b e) -> p b e", e=NE)
        be = sb("be", [1, MAXBLK])
        be2 = sb("be2", [1, MAXBLK])

        (s_v, s_exp, s_dv, s_hot, s_rank, s_onehots, s_slots, s_idx, s_be, s_nf) = (k.sem("m_" + n) for n in (
            "dve", "exp", "dexp", "onehots", "rank_ps", "slot_onehots", "slots_ps", "slots", "blocks", "norm_f"))
        s_w1, s_w3, s_w2, s_g, s_ys = ([k.sem(f"m_{n}{i}") for i in range(2)] for n in (
            "w1_", "w3_", "w2_", "gathered", "stored"))
        (s_gp, s_up, s_xt, s_ht, s_y, s_silu, s_hh, s_hc, s_xe, s_yo, s_copied) = (k.sem("m_" + n) for n in (
            "gate_ps", "up_ps", "x_turned", "h_turned", "y_ps", "silu", "hidden", "hT", "xT", "y", "idx_copied"))
        s_ya = [k.sem(f"m_rows{t}") for t in range(NT)]
        s_fs = k.sem("m_final")
        s_add, s_ss, s_var, s_std, s_rstd, s_fin = (k.sem("m_" + n) for n in (
            "added", "ss", "var", "std", "rstd", "fin"))
        s_passed = k.sem("m_pool_passed")
        block = k.block(mem)
        HALF = MAXBLK // 2

        def used(eng):
            eng.wait_ge(s_be, 2)
            return eng.value_load(nb_i[0:1, 0:1], min_val=2 * S // P, max_val=MAXBLK - 1)

        @block.sync
        def _(sp):
            sp.dma_start(nf[:, :], k.norm_f.partition_broadcast(P)).then_inc(s_nf, 16)
            n = used(sp)
            with sp.Fori(0, HALF) as i:
                for s in range(2):
                    with sp.If(2 * i + s < n):
                        e = sp.value_load(be_i[0:1, bass.ds(2 * i + s, 1)], min_val=0, max_val=NE - 1)
                        sp.wait_ge(s_up, 2 * i + (s + 1))
                        sp.dma_start(w1[s][:, :, :], k.exp_w1[0, bass.ds(e, 1)].rearrange(
                            "e (k p) n -> p (e k) n", p=P)).then_inc(s_w1[s], 16)
                        sp.dma_start(w3[s][:, :, :], k.exp_w3[0, bass.ds(e, 1)].rearrange(
                            "e (k p) n -> p (e k) n", p=P)).then_inc(s_w3[s], 16)
                        sp.wait_ge(s_y, 2 * i + (s + 1))
                        sp.dma_start(w2[s][:, :, :], k.exp_w2[0, bass.ds(e, 1)].rearrange(
                            "e (k p) n -> p (e k) n", p=P)).then_inc(s_w2[s], 16)
            for t in range(NT):
                sp.wait_ge(s_fin, t + 1)
                sp.dma_start(k.out[0, t * P:(t + 1) * P, :], ya[t]).then_inc(s_fs, 16)
            sp.wait_ge(s_fs, 16 * NT)

        @block.gpsimd
        def _(pool):
            pool.wait_ge(s_idx, 1)

            def gather(s, col):
                pool.tensor_copy(idxs[s][:, :], slot_i[:, bass.ds(col, 1)]).then_inc(s_copied, 1)
                pool.wait_ge(s_copied, col + 1)
                settle(pool, s_passed)
                pool.indirect_dma_start(xg[s][:, :], None, k.d_xn, bass.IndirectOffsetOnAxis(ap=idxs[s][:, 0:1], axis=0),
                                        bounds_check=S - 1, oob_is_err=True).then_inc(s_g[s], 16)

            gather(0, 0)
            n = used(pool)
            with pool.Fori(0, HALF) as i:
                for s in range(2):
                    with pool.If(2 * i + s < n):
                        pool.wait_ge(s_xt, 2 * i + (s + 1))
                        settle(pool, s_passed)
                        gather(1 - s, 2 * i + (s + 1))
            pool.wait_ge(s_ys[0], 16 * ((n + 1) // 2) + 16)
            pool.wait_ge(s_ys[1], 16 * (n // 2) + 16)
            settle(pool, s_passed)
            for t in range(NT):
                for dst, j in ((ya, 0), (yb, 1)):
                    pool.indirect_dma_start(dst[t], None, k.d_y,
                                            bass.IndirectOffsetOnAxis(ap=dest_i[:, j, t:t + 1], axis=0),
                                            bounds_check=MAXBLK * P - 1, oob_is_err=True).then_inc(s_ya[t], 16)

        @block.scalar
        def _(act):
            for s in range(2):
                act.sem_inc(s_ys[s], 16)
            act.sem_inc(s_silu, 1)
            act.sem_inc(s_xe, 1)
            act.wait_ge(s_v, 2)
            act.activation(el[:, :, :], dl[:, :, :], ACT.Exp).then_inc(s_exp, 1)
            act.wait_ge(s_dv, 1)
            act.activation(ev[:, :], dv[:, :], ACT.Exp).then_inc(s_exp, 1)

            def modulate(s):
                for kk in range(KD):
                    last = act.activation(xT[s][:, kk, :], k.psum[:, 2 + kk // 4, (kk % 4) * P:(kk % 4 + 1) * P],
                                          ACT.Identity, scale=k.modA[:, 1, kk:kk + 1], bias=k.mod[:, 24 + kk:25 + kk])
                last.then_inc(s_xe, 1)

            act.wait_ge(s_xt, 2)
            modulate(0)
            n = used(act)
            with act.Fori(0, HALF) as i:
                for s in range(2):
                    with act.If(2 * i + s < n):
                        act.wait_ge(s_gp, 2 * i + (s + 1))
                        act.wait_ge(s_hh, 2 * i + (s + 1))
                        act.activation(sg[s][:, :], k.psum[:, 0, :], ACT.Silu).then_inc(s_silu, 1)
                        act.wait_ge(s_xt, 2 * i + (s + 3))
                        modulate(1 - s)
                        act.wait_ge(s_yo, 2 * i + (s + 1 + 1))
                        act.dma_start(k.d_y[bass.ds((2 * i + s) * P, P), :], ys[s]).then_inc(s_ys[s], 16)
            for t in range(NT + 1):
                if t < NT:
                    act.wait_ge(s_add, 2 * t + 2)
                    if t >= 2:
                        act.wait_ge(s_ss, t - 1)
                    act.activation(ys[t % 2], x2[:, t, :], ACT.Square, accum_out=ss[:, t:t + 1]).then_inc(s_ss, 1)
                if t >= 1:
                    act.wait_ge(s_var, t)
                    act.activation(std[:, t - 1:t], var[:, t - 1:t], ACT.Sqrt).then_inc(s_std, 1)

        @block.vector
        def _(dve):
            const = lambda c, n: k.const[:, c:c + n]
            v = Count(s_v)
            tt, red = dve.tensor_tensor, dve.tensor_reduce
            lg = logits[:, :, 0:NG]
            v.inc(red(gmax[:, :], lg, AX, ALU.max)); v.wait(dve)
            v.inc(tt(dl[:, :, :], lg, gmax[:, :].unsqueeze(2).to_broadcast([P, NT, NG]), ALU.subtract)); v.wait(dve)
            v.inc(dve.tensor_scalar(eq[:, :, :], dl[:, :, :], 0.0, -4.0, ALU.is_equal, ALU.mult)); v.wait(dve)
            v.inc(tt(cand[:, :, :], eq[:, :, :], const(K_G4, NG).unsqueeze(1).to_broadcast([P, NT, NG]), ALU.add))
            v.wait(dve)
            v.inc(red(gm_[:, :], cand[:, :, :], AX, ALU.min)); v.wait(dve)
            v.inc(tt(one[:, :, :], cand[:, :, :], gm_[:, :].unsqueeze(2).to_broadcast([P, NT, NG]), ALU.is_equal))
            v.wait(dve)
            v.inc(dve.tensor_scalar(gmask[:, :, :], one[:, :, :], -MASKED, MASKED, ALU.mult, ALU.add)); v.wait(dve)
            v.inc(tt(lem[:, :, :].rearrange("p t (g e) -> p t g e", g=NG),
                     logits[:, :, NG:].rearrange("p t (g e) -> p t g e", g=NG),
                     gmask[:, :, :].unsqueeze(3).to_broadcast([P, NT, NG, EPG]), ALU.add))
            v.wait(dve)
            for t in range(NT):
                v.inc(dve.max(top[:, t, :], lem[:, t, :]))
            v.wait(dve)
            for t in range(NT):
                v.inc(dve.max_index(topi[:, t, :], top[:, t, :], lem[:, t, :]))
            tt(dv[:, :], top[:, :, 1], top[:, :, 0], ALU.subtract).then_inc(s_dv, 1)
            v.wait(dve)
            v.inc(dve.tensor_copy(ef[:, :, :], topi[:, :, 0:2])); v.wait(dve)
            e32 = const(K_E32, NE).unsqueeze(1).to_broadcast([P, NT, NE])
            for j in range(2):
                v.inc(tt(hot[:, j], e32, ef[:, :, j].unsqueeze(2).to_broadcast([P, NT, NE]), ALU.is_equal))
            v.wait(dve)
            tt(both[:, :, :], hot[:, 0], hot[:, 1], ALU.add).then_inc(s_hot, 1)
            dve.wait_ge(s_exp, 2)
            v.inc(red(se[:, :], el[:, :, :], AX, ALU.add))
            v.inc(dve.tensor_scalar(es[:, :], ev[:, :], 1.0, None, ALU.add)); v.wait(dve)
            v.inc(dve.reciprocal(pg[:, :], se[:, :]))
            v.inc(dve.reciprocal(er[:, :], es[:, :])); v.wait(dve)
            v.inc(tt(wts[:, 0], er[:, :], pg[:, :], ALU.mult)); v.wait(dve)
            v.inc(tt(wts[:, 1], wts[:, 0], ev[:, :], ALU.mult))
            dve.wait_ge(s_rank, 1)
            v.inc(dve.tensor_copy(cnt[:, :], k.psum[:, 1, 0:NE])); v.wait(dve)
            v.inc(tt(over[:, :, :], cnt[:, :].unsqueeze(2).to_broadcast([P, NE, NT]),
                     const(K_M128, NT).unsqueeze(1).to_broadcast([P, NE, NT]), ALU.is_gt)); v.wait(dve)
            v.inc(red(nb[:, :], over[:, :, :], AX, ALU.add)); v.wait(dve)
            v.inc(dve.tensor_tensor_scan(end[:, :], const(K_ONE, NE), nb[:, :], 0.0, ALU.mult, ALU.add)); v.wait(dve)
            v.inc(tt(ended[:, :, :], end[0:1, :].unsqueeze(1).to_broadcast([1, MAXBLK, NE]),
                     k.const[0:1, K_BLK:K_BLK + MAXBLK].unsqueeze(2).to_broadcast([1, MAXBLK, NE]), ALU.is_le))
            v.inc(tt(start[:, :], end[:, :], nb[:, :], ALU.subtract)); v.wait(dve)
            v.inc(red(be[:, :], ended[:, :, :], AX, ALU.add)); v.wait(dve)
            dve.tensor_scalar(be_i[:, :], be[:, :], float(NE - 1), None, ALU.min).then_inc(s_be, 1)
            dve.tensor_copy(nb_i[:, :], end[0:1, NE - 1:NE]).then_inc(s_be, 1)
            v.inc(dve.scalar_tensor_tensor(base[:, :, :], start[:, :].unsqueeze(1).to_broadcast([P, NT, NE]), float(P),
                                           k.psum[:, 0, 0:NT * NE].rearrange("p (t e) -> p t e", t=NT),
                                           ALU.mult, ALU.add)); v.wait(dve)
            for j in range(2):
                v.inc(tt(pick[:, j], hot[:, j], base[:, :, :], ALU.mult))
            v.wait(dve)
            v.inc(red(dest[:, :, :], pick[:, :, :, :], AX, ALU.add)); v.wait(dve)
            v.inc(dve.tensor_copy(dest_i[:, :, :], dest[:, :, :]))
            flat = dest[:, :, :].rearrange("p j t -> p (j t)")
            b49 = const(K_B128, MAXBLK + 1).unsqueeze(1).to_broadcast([P, 2 * NT, MAXBLK + 1])
            v.inc(tt(ge[:, :, :], flat.unsqueeze(2).to_broadcast([P, 2 * NT, MAXBLK + 1]), b49, ALU.is_ge)); v.wait(dve)
            v.inc(red(blkno[:, :, :].rearrange("p j t -> p (j t)"), ge[:, :, :], AX, ALU.add))
            v.inc(tt(inblk[:, :, :], ge[:, :, 0:MAXBLK], ge[:, :, 1:MAXBLK + 1], ALU.subtract)); v.wait(dve)
            v.inc(dve.scalar_tensor_tensor(row[:, :, :], blkno[:, :, :], -float(P), dest[:, :, :], ALU.mult, ALU.add))
            tok = const(K_TOK, NT).unsqueeze(2).to_broadcast([P, NT, MAXBLK])
            for j in range(2):
                v.inc(tt(inblk[:, NT * j:NT * (j + 1), :], inblk[:, NT * j:NT * (j + 1), :], tok, ALU.mult))
            v.wait(dve)
            dve.scalar_tensor_tensor(rowhot[:, :, :], row[:, :, :].rearrange("p j t -> p (j t)").unsqueeze(2)
                                     .to_broadcast([P, 2 * NT, P]), float(P),
                                     const(K_I128, P).unsqueeze(1).to_broadcast([P, 2 * NT, P]),
                                     ALU.add, ALU.is_equal).then_inc(s_onehots, 1)
            dve.wait_ge(s_slots, 1)
            dve.tensor_copy(slot_i[:, 0:MAXBLK], k.psum[:, 4, 0:MAXBLK]).then_inc(s_idx, 1)

            dve.sem_inc(s_hh, 1)
            dve.sem_inc(s_yo, 1)
            n = used(dve)
            with dve.Fori(0, HALF) as i:
                for s in range(2):
                    with dve.If(2 * i + s < n):
                        dve.wait_ge(s_silu, 2 * i + (s + 2))
                        dve.wait_ge(s_up, 2 * i + (s + 3))
                        dve.tensor_tensor(hh[s][:, :], k.psum[:, 1, :], sg[s][:, :], ALU.mult).then_inc(s_hh, 1)
                        dve.wait_ge(s_ht, 2 * i + (s + 1))
                        dve.tensor_copy(hT[s][:, :, :].rearrange("p a b -> p (a b)"), k.psum[:, 4, :]).then_inc(s_hc, 1)
                        dve.wait_ge(s_y, 2 * i + (s + 3))
                        dve.wait_ge(s_ys[s], 16 * i + 16)
                        dve.tensor_tensor(ys[s], k.psum[:, 5:7, :].rearrange("p a b -> p (a b)"), g2row[:, :],
                                          ALU.mult).then_inc(s_yo, 1)
            dve.wait_ge(s_nf, 16)
            for t in range(NT + 1):
                if t < NT:
                    dve.wait_ge(s_ya[t], 32)
                    dve.scalar_tensor_tensor(x2[:, t, :], ya[t], wts[:, 0, t:t + 1], x2[:, t, :],
                                             ALU.mult, ALU.add).then_inc(s_add, 1)
                    dve.wait_ge(s_add, 2 * t + 1)
                    dve.scalar_tensor_tensor(x2[:, t, :], yb[t], wts[:, 1, t:t + 1], x2[:, t, :],
                                             ALU.mult, ALU.add).then_inc(s_add, 1)
                if t >= 1:
                    u, col = t - 1, slice(t - 1, t)
                    dve.wait_ge(s_ss, u + 1)
                    dve.tensor_scalar(var[:, col], ss[:, col], 1.0 / D, EPS, ALU.mult, ALU.add).then_inc(s_var, 1)
                    dve.wait_ge(s_std, u + 1)
                    dve.reciprocal(rstd[:, col], std[:, col]).then_inc(s_rstd, 1)
                    dve.wait_ge(s_rstd, u + 1)
                    dve.scalar_tensor_tensor(ya[u], x2[:, u, :], rstd[:, col], nf[:, :], ALU.mult, ALU.mult
                                             ).then_inc(s_fin, 1)

        @block.tensor
        def _(pe):
            pe.sem_inc(s_up, 2)
            pe.sem_inc(s_y, 2)
            pe.sem_inc(s_xt, 1)
            pe.wait_ge(s_hot, 1)
            ones, tri = k.const[:, K_ONE:K_ONE + P], k.const[:, K_TRI:K_TRI + P]
            for t in range(NT):
                for j in range(t + 1):
                    pe.matmul(k.psum[:, 0, t * NE:(t + 1) * NE], tri if j == t else ones, both[:, j, :],
                              start=(j == 0), stop=(j == t))
            for t in range(NT):
                mm = pe.matmul(k.psum[:, 1, 0:NE], ones, both[:, t, :], start=(t == 0), stop=(t == NT - 1))
            mm.then_inc(s_rank, 1)
            pe.wait_ge(s_onehots, 1)
            for j in range(2 * NT):
                mm = pe.matmul(k.psum[:, 4, 0:MAXBLK], rowhot[:, j, :], inblk[:, j, :],
                               start=(j == 0), stop=(j == 2 * NT - 1))
            mm.then_inc(s_slots, 1)

            def turn(s):
                for kk in range(KD):
                    tr = pe.transpose(k.psum[:, 2 + kk // 4, (kk % 4) * P:(kk % 4 + 1) * P],
                                      xg[s][:, kk * P:(kk + 1) * P], k.ident)
                tr.then_inc(s_xt, 1)

            pe.wait_ge(s_g[0], 16)
            turn(0)
            n = used(pe)
            with pe.Fori(0, HALF) as i:
                for s in range(2):
                    with pe.If(2 * i + s < n):
                        pe.wait_ge(s_xe, 2 * i + (s + 2))
                        pe.wait_ge(s_silu, 2 * i + (s + 1))
                        pe.wait_ge(s_w1[s], 16 * i + 16)
                        for kk in range(KD):
                            mm = pe.matmul(k.psum[:, 0, :], xT[s][:, kk, :], w1[s][:, kk, :],
                                           start=(kk == 0), stop=(kk == KD - 1))
                        mm.then_inc(s_gp, 1)
                        pe.wait_ge(s_hh, 2 * i + (s + 1))
                        pe.wait_ge(s_w3[s], 16 * i + 16)
                        for kk in range(KD):
                            mm = pe.matmul(k.psum[:, 1, :], xT[s][:, kk, :], w3[s][:, kk, :],
                                           start=(kk == 0), stop=(kk == KD - 1))
                        mm.then_inc(s_up, 1)
                        pe.wait_ge(s_g[1 - s], 16 * i + 16 * (s + 1) if s else 16 * i + 16)
                        turn(1 - s)
                        pe.wait_ge(s_hh, 2 * i + (s + 2))
                        for c in range(KE):
                            tr = pe.transpose(k.psum[:, 4, c * P:(c + 1) * P], hh[s][:, c * P:(c + 1) * P], k.ident)
                        tr.then_inc(s_ht, 1)
                        pe.wait_ge(s_hc, 2 * i + (s + 1))
                        pe.wait_ge(s_yo, 2 * i + (s + 1))
                        pe.wait_ge(s_w2[s], 16 * i + 16)
                        for half in range(2):
                            for c in range(KE):
                                mm = pe.matmul(k.psum[:, 5 + half, :], hT[s][:, c, :],
                                               w2[s][:, c, half * BANK:(half + 1) * BANK],
                                               start=(c == 0), stop=(c == KE - 1))
                        mm.then_inc(s_y, 1)


def build(nc, args):
    with ExitStack() as ctx:
        k = Core(nc, ctx, args)
        s_cw, s_wo = k.sem("cmp_weights"), k.sem("w_o")
        k.stage_sems.clear()
        rows = k.sbuf(ctx, "rows", [P, KD, S])
        logits = k.sbuf(ctx, "logits", [P, NT, NG + NE])
        g2row = k.sbuf(ctx, "g2row", [P, D])
        stage_condition_and_norm(k, rows)
        with ExitStack() as mix:
            oT = k.sbuf(mix, "oT", [P, 6, S])
            with ExitStack() as att:
                o_nsa = k.sbuf(att, "o_nsa", [P, NT, NSA_H * DH])
                with ExitStack() as kv:
                    vA = k.sbuf(kv, "vA", [P, NT, RV])
                    vD = k.sbuf(kv, "vD", [P, DIL_G, NT, 256])
                    gates = k.sbuf(kv, "gates", [P, NT, 3 * NSA_H])
                    kc = k.sbuf(kv, "kc", [P, 2, NSA_KV * NC])
                    vc = k.sbuf(kv, "vc", [P, NSA_KV, DH])
                    with ExitStack() as cw:
                        w1c = k.sbuf(cw, "w1c", [P, 2, LP, CMP_HID])
                        w2c = k.sbuf(cw, "w2c", [P, 2, 2, DH])
                        stage_projections(k, rows, vA, vD, gates, w1c, w2c, s_cw)
                        stage_compress(k, w1c, w2c, s_cw, kc, vc)
                    stage_nsa(k, vA, gates, kc, vc, o_nsa)
                    stage_dilated(k, vD)
                stage_join(k, o_nsa, oT)
            mT = k.sbuf(mix, "mT", [P, KD, S])
            acc = k.sbuf(mix, "acc", [P, 4 * D])
            g1row = k.sbuf(mix, "g1row", [P, D])
            w_o = k.sbuf(mix, "w_o_sb", [P, KD, D])
            stage_merge(k, rows, oT, mT, acc, g1row, g2row, w_o, s_wo)
            stage_out(k, mT, g1row, w_o, rows, logits, s_wo)
        stage_moe(k, rows, logits, g2row)


def kernel(**inputs):
    import numpy as _np
    import concourse.bacc as _bacc
    from concourse import mybir as _mybir
    from concourse.bass_utils import run_bass_kernel_spmd as _run

    nc = _bacc.Bacc("TRN2", target_bir_lowering=False, num_devices=1)
    given = {name: inputs[name] for name in INPUTS}
    given["c_small"], given["c_onehot"] = shape_constants()
    arrays, args = {}, {}
    for name, value in given.items():
        a = _np.ascontiguousarray(value)
        arrays[f"in_{name}_dram"] = a
        args[name] = nc.dram_tensor(f"in_{name}_dram", a.shape, _mybir.dt.from_np(a.dtype), kind="ExternalInput").ap()
    args["out"] = nc.dram_tensor("out_0_dram", (1, S, D), _mybir.dt.float32, kind="ExternalOutput").ap()
    build(nc, args)
    r = _run(nc, [arrays], core_ids=[0])
    return r.results[0]["out_0_dram"]
```
